# Optimizing a Trainium2 kernel written in Bass

```python
import math
import jax, jax.numpy as jnp
from jax import lax
import numpy as np

D_MODEL = 2048
BATCH = 1
SEQ = 256
DEPTH = 2

CHUNK = 64
Q_BLOCK = 128
ROPE_THETA = 10000.0
EPS = 1e-6
NEG = -1e30
D_MIX = D_MODEL
D_FF = 4 * D_MODEL

A_HEADS = 4
A_DQK = D_MIX // 16
A_DV = 2 * A_DQK
A_WIDTH = A_HEADS * A_DV

B_GROUPS = 4
B_CH = D_MIX // 16
B_WIDTH = B_GROUPS * B_CH
B_BLOCK = 128

C_HEADS = 4
C_DH = D_MIX // 16
C_WIDTH = C_HEADS * C_DH
IDX_HEADS = 8
IDX_DH = D_MIX // 32
TOPK_MAX = 256

IN_SIZES = (
    A_HEADS * 2 * A_DQK,
    A_HEADS * 2 * A_DQK,
    A_HEADS * A_DV,
    B_WIDTH,
    B_WIDTH,
    C_WIDTH,
    C_WIDTH,
    C_WIDTH,
    IDX_HEADS * IDX_DH,
    IDX_DH,
    IDX_HEADS,
)
N_IN = sum(IN_SIZES)

kernel_name = "hybrid_diffattn_gmlp_dsa_trunk"

def rms_norm(x, gain=None):
    xf = x.astype(jnp.float32)
    y = xf * lax.rsqrt(jnp.mean(xf * xf, axis=-1, keepdims=True) + EPS)
    if gain is not None:
        y = y * gain.astype(jnp.float32)
    return y.astype(x.dtype)

def rope_tables(seq, dim, dtype):
    inv = 1.0 / (ROPE_THETA ** (jnp.arange(0, dim, 2, dtype=jnp.float32) / dim))
    ang = jnp.arange(seq, dtype=jnp.float32)[:, None] * inv[None, :]
    ang = jnp.concatenate([ang, ang], axis=-1)
    return jnp.cos(ang).astype(dtype), jnp.sin(ang).astype(dtype)

def apply_rope(x, cos, sin):
    shape = (x.shape[1],) + (1,) * (x.ndim - 3) + (x.shape[-1],)
    half = x.shape[-1] // 2
    rot = jnp.concatenate([-x[..., half:], x[..., :half]], axis=-1)
    return x * cos.reshape(shape) + rot * sin.reshape(shape)

def to_blocks(t):
    b, s = t.shape[:2]
    return jnp.moveaxis(t.reshape((b, s // Q_BLOCK, Q_BLOCK) + t.shape[2:]), 1, 0)

def from_blocks(t):
    t = jnp.moveaxis(t, 0, 1)
    return t.reshape((t.shape[0], t.shape[1] * t.shape[2]) + t.shape[3:])

def diff_attention(q, k, v, lam, lambda_init, subln_gain):
    S = q.shape[1]
    scale = q.shape[-1] ** -0.5
    key_chunk = jnp.arange(S) // CHUNK
    starts = jnp.arange(S // Q_BLOCK) * Q_BLOCK

    def one_block(args):
        qb, start = args
        s = jnp.einsum('bqhmd,bshmd->bmhqs', qb, k).astype(jnp.float32) * scale
        q_chunk = (start + jnp.arange(Q_BLOCK)) // CHUNK
        mask = key_chunk[None, :] <= q_chunk[:, None]
        p = jax.nn.softmax(jnp.where(mask, s, NEG), axis=-1)
        a = p[:, 0] - lam * p[:, 1]
        return jnp.einsum('bhqs,bshe->bqhe', a.astype(v.dtype), v)

    o = from_blocks(lax.map(one_block, (to_blocks(q), starts)))
    return rms_norm(o, subln_gain) * (1.0 - lambda_init)

def spatial_gating(u, v, v_gain, ws, bias):
    b, S = u.shape[:2]
    v = rms_norm(v.reshape(b, S, B_GROUPS, B_CH), v_gain.reshape(B_GROUPS, B_CH))
    v = v.reshape(b, S // B_BLOCK, B_BLOCK, B_GROUPS, B_CH)
    pos_chunk = jnp.arange(B_BLOCK) // CHUNK
    mask = pos_chunk[None, :] <= pos_chunk[:, None]
    w = jnp.where(mask[None], ws, 0.0).astype(v.dtype)
    z = jnp.einsum('gij,bnjgc->bnigc', w, v) + bias.T[None, None, :, :, None]
    return u * z.reshape(b, S, B_WIDTH)

def dsa_attention(q, k, v, qi, ki, wi, topk):
    b, S = q.shape[:2]
    scale = q.shape[-1] ** -0.5
    key_chunk = jnp.arange(S) // CHUNK
    starts = jnp.arange(S // Q_BLOCK) * Q_BLOCK
    bidx = jnp.arange(b)[:, None, None]

    def one_block(args):
        qb, qib, wib, start = args
        q_chunk = (start + jnp.arange(Q_BLOCK)) // CHUNK
        mask = key_chunk[None, :] <= q_chunk[:, None]
        iscore = jnp.einsum('bqhd,bsd->bqhs', qib, ki).astype(jnp.float32)
        iscore = jnp.einsum('bqhs,bqh->bqs', jax.nn.relu(iscore), wib.astype(jnp.float32))
        iscore = jnp.where(mask[None], iscore, NEG)
        top_val, top_idx = lax.top_k(iscore, topk)
        valid = top_val > 0.5 * NEG
        kg = k[bidx, top_idx]
        vg = v[bidx, top_idx]
        s = jnp.einsum('bqhd,bqkhd->bhqk', qb, kg).astype(jnp.float32) * scale
        p = jax.nn.softmax(jnp.where(valid[:, None], s, NEG), axis=-1)
        return jnp.einsum('bhqk,bqkhd->bqhd', p.astype(vg.dtype), vg)

    return from_blocks(lax.map(one_block, (to_blocks(q), to_blocks(qi), to_blocks(wi), starts)))

def setup_inputs(seed: int = 0) -> dict:
    key = jax.random.key(seed)
    ks = jax.random.split(key, 17)

    def nrm(k, shape, s):
        return jax.random.normal(k, shape, jnp.float32) * s

    L = DEPTH
    return {
        "x": nrm(ks[0], (BATCH, SEQ, D_MODEL), 1.0),
        "c": nrm(ks[1], (BATCH, D_MODEL), 1.0),
        "w_mod": nrm(ks[2], (L, D_MODEL, 6 * D_MODEL), 0.5 * D_MODEL ** -0.5),
        "b_mod": nrm(ks[3], (L, 6 * D_MODEL), 0.01),
        "w_in": nrm(ks[4], (L, D_MODEL, N_IN), D_MODEL ** -0.5),
        "w_out": nrm(ks[5], (L, D_MIX, D_MODEL), D_MIX ** -0.5),
        "a_qnorm": 1.0 + nrm(ks[6], (L, A_DQK), 0.05),
        "a_knorm": 1.0 + nrm(ks[7], (L, A_DQK), 0.05),
        "a_lambda": nrm(ks[8], (L, 4, A_DQK), 0.1),
        "a_subln": 1.0 + nrm(ks[9], (L, A_DV), 0.05),
        "b_vnorm": 1.0 + nrm(ks[10], (L, B_WIDTH), 0.05),
        "b_ws": nrm(ks[11], (L, B_GROUPS, B_BLOCK, B_BLOCK), B_BLOCK ** -0.5),
        "b_bias": 1.0 + nrm(ks[12], (L, B_GROUPS, B_BLOCK), 0.1),
        "c_qnorm": 1.0 + nrm(ks[13], (L, C_DH), 0.05),
        "c_knorm": 1.0 + nrm(ks[14], (L, C_DH), 0.05),
        "w_ff1": nrm(ks[15], (L, D_MODEL, D_FF), D_MODEL ** -0.5),
        "w_ff2": nrm(ks[16], (L, D_FF, D_MODEL), D_FF ** -0.5),
    }

def reference(x, c, w_mod, b_mod, w_in, w_out, a_qnorm, a_knorm, a_lambda, a_subln,
              b_vnorm, b_ws, b_bias, c_qnorm, c_knorm, w_ff1, w_ff2):
    B, S, _ = x.shape
    topk = min(TOPK_MAX, S // 4)
    cos128, sin128 = rope_tables(S, A_DQK, x.dtype)
    cos64, sin64 = rope_tables(S, IDX_DH, x.dtype)
    offs = []
    acc = 0
    for n in IN_SIZES[:-1]:
        acc += n
        offs.append(acc)
    c_act = jax.nn.silu(c)

    for l in range(DEPTH):
        lambda_init = 0.8 - 0.6 * math.exp(-0.3 * l)
        mod = jnp.einsum('bd,de->be', c_act, w_mod[l]) + b_mod[l]
        sh1, sc1, g1, sh2, sc2, g2 = jnp.split(mod[:, None, :], 6, axis=-1)

        h = rms_norm(x) * (1.0 + sc1) + sh1
        proj = jnp.einsum('bsd,de->bse', h, w_in[l])
        aq, ak, av, bu, bv, cq, ck, cv, iq, ik, iw = jnp.split(proj, offs, axis=-1)

        aq = apply_rope(rms_norm(aq.reshape(B, S, A_HEADS, 2, A_DQK), a_qnorm[l]), cos128, sin128)
        ak = apply_rope(rms_norm(ak.reshape(B, S, A_HEADS, 2, A_DQK), a_knorm[l]), cos128, sin128)
        lam_p = a_lambda[l].astype(jnp.float32)
        lam = (jnp.exp(jnp.sum(lam_p[0] * lam_p[1])) - jnp.exp(jnp.sum(lam_p[2] * lam_p[3]))
               + lambda_init)
        oa = diff_attention(aq, ak, av.reshape(B, S, A_HEADS, A_DV), lam, lambda_init, a_subln[l])

        ob = spatial_gating(jax.nn.gelu(bu), jax.nn.gelu(bv), b_vnorm[l], b_ws[l], b_bias[l])

        cq = apply_rope(rms_norm(cq.reshape(B, S, C_HEADS, C_DH), c_qnorm[l]), cos128, sin128)
        ck = apply_rope(rms_norm(ck.reshape(B, S, C_HEADS, C_DH), c_knorm[l]), cos128, sin128)
        iq = apply_rope(iq.reshape(B, S, IDX_HEADS, IDX_DH), cos64, sin64)
        ik = apply_rope(ik, cos64, sin64)
        iw = iw * (IDX_HEADS ** -0.5 * IDX_DH ** -0.5)
        oc = dsa_attention(cq, ck, cv.reshape(B, S, C_HEADS, C_DH), iq, ik, iw, topk)

        mix = jnp.concatenate([oa.reshape(B, S, A_WIDTH), ob, oc.reshape(B, S, C_WIDTH)], axis=-1)
        x = x + g1 * jnp.einsum('bse,ed->bsd', mix, w_out[l])

        h = rms_norm(x) * (1.0 + sc2) + sh2
        ff = jnp.square(jax.nn.relu(jnp.einsum('bsd,df->bsf', h, w_ff1[l])))
        x = x + g2 * jnp.einsum('bsf,fd->bsd', ff, w_ff2[l])

    return x


_drawn_inputs = setup_inputs


def setup_inputs(seed=0):
    import zlib

    import numpy as np

    out = dict(_drawn_inputs(seed))
    spreads = {}
    factors = {'a_qnorm': 8.0,
     'a_knorm': 8.0,
     'a_subln': 4.952,
     'b_vnorm': 8.0,
     'b_bias': 3.747,
     'c_qnorm': 8.0,
     'c_knorm': 8.0}
    for name, (base, spread) in spreads.items():
        noise = np.random.default_rng([zlib.crc32(name.encode()), seed]).standard_normal(out[name].shape)
        drawn = base * np.exp(spread * noise) if base else spread * noise
        out[name] = __import__('jax').numpy.asarray(drawn.astype(out[name].dtype))
    for name, factor in factors.items():
        out[name] = (out[name] * factor).astype(out[name].dtype)
    return out
```

```python
import math
from contextlib import ExitStack

import numpy as np

import concourse.bass as bass
from concourse import mybir

F32 = mybir.dt.float32
F32R = mybir.dt.float32r
I32 = mybir.dt.int32
ACT = mybir.ActivationFunctionType
ALU = mybir.AluOpType
AX = mybir.AxisListType

P = 128
D = 2048
S = 256
T = S // P
KT = D // P
DEPTH = 2
D_FF = 4 * D
CHUNK = 64
EPS = 1e-6
NEG = -1e30
TAKEN = -3e38
TOPK = S // 4
DH = 128
IDX_HEADS, IDX_DH = 8, 64
N = 512
UNIT_KT = 2
UNITS = KT // UNIT_KT
RAW_SLOTS, SPLIT_SLOTS, MOD_SLOTS = 4, 4, 4
AHEAD = SPLIT_SLOTS - 2
MODW = 1024
HALF_TILES = KT
QK_SCALE = DH ** -0.5
IDX_SCALE = IDX_HEADS ** -0.5 * IDX_DH ** -0.5
GELU_A, GELU_B = 0.044715, math.sqrt(2.0 / math.pi)

IN_CHUNKS = {
    "ik": (6144, 72), "iq": (5632, N), "ck": (4608, N), "cq": (4096, N), "cv": (5120, N),
    "ak0": (1024, N), "aq0": (0, N), "av0": (2048, N),
    "ak1": (1536, N), "aq1": (512, N), "av1": (2560, N), "bv": (3584, N), "bu": (3072, N),
}
IN_NAMES = list(IN_CHUNKS)
N_IN_CHUNKS = len(IN_NAMES)
N_OUT_CHUNKS = D // N
UP = D // N
ROUNDS = D_FF // D
IN_UNITS = N_IN_CHUNKS * UNITS
STRAIGHT_UNITS = IN_UNITS + N_OUT_CHUNKS * UNITS
ROUND_UNITS = 2 * UP * UNITS
LAYER_UNITS = STRAIGHT_UNITS + ROUNDS * ROUND_UNITS
LAYER_CHUNKS = LAYER_UNITS // UNITS
LAYER_ACT_CHUNKS = N_IN_CHUNKS + ROUNDS * UP
LAYER_DVE_CHUNKS = N_OUT_CHUNKS + ROUNDS * UP

KT_C, KT_A0, KT_B, KT_A1 = 12, 0, 8, 4
def _out_units():
    early = [KT_C, KT_C + 2, KT_A0, KT_A0 + 2]
    late = [KT_B, KT_B + 2, KT_A1, KT_A1 + 2]
    units = []
    for part in (early, late):
        for j in (0, 1):
            units += [(j, k, part is early and k == early[0], part is late and k == late[-1]) for k in part]
    for j in (2, 3):
        units += [(j, k, k == early[0], k == late[-1]) for k in early + late]
    return units
OUT_UNITS = _out_units()

SH1, SC1, G1, SH2, SC2, G2 = range(6)
def mod_plan(l):
    params = [G1, SH2, SC2, G2] if l == 0 else [SC2, G2]
    return [(p, h, UNITS + (2 * i + h) * HALF_TILES) for i, p in enumerate(params) for h in (0, 1)]
ROUND_PARAMS = [SH1, SC1, G1, SH2]
HALVES_BEFORE = [4, 4 + len(mod_plan(0)) + 2 * ROUNDS]

ROPED = ["ck", "cq", "ak0", "aq0", "ak1", "aq1"]
def evac_at(name):
    return IN_NAMES.index(name) * UNITS + UNITS + 1
GROUPS = {"C": 46, "A0": 67, "A1": 91}

def _steps():
    pe, act, dve = [], [], []
    pe += [("T_ws", 2)]
    dve += [("ws_mask", 2), ("ws", 4)]
    pe += [("T_ik", 12), ("T_iq", 21), ("idx0", 23), ("idx1", 28), ("idx2", 31)]
    act += [("ev_ik", 9), ("tv_ik", 13), ("ev_iq", 17), ("tv_iq", 22)]
    dve += [("rope_ik", 9), ("rope_iq", 19), ("isc0", 27), ("isc1", 30), ("isc2", 32)]
    dve += [("topk0", 41), ("topk1", 46), ("mask", 47), ("maskA", 66)]
    for c in ROPED:
        e = evac_at(c)
        act += [("ev_" + c, e), ("tv_" + c, e + 5)]
        dve += [("rs_" + c, e), ("mul_" + c, e + 1), ("rope_" + c, e + 3)]
        pe += [("T_" + c, e + 4)]
    for c in ("cv", "av0", "av1"):
        act += [("ev_" + c, evac_at(c))]
    for g, b in GROUPS.items():
        for t, o in ((0, 0), (1, 6)):
            pe += [(f"s{g}{t}", b + o), (f"p{g}{t}", b + o + 5), (f"o{g}{t}", b + o + 8)]
            dve += [(f"m{g}{t}", b + o + 2)]
            act += [(f"e{g}{t}", b + o + 3), (f"t{g}{t}", b + o + 6), (f"v{g}{t}", b + o + 10)]
            if g == "C":
                dve += [(f"i{g}{t}", b + o + 4)]
            else:
                dve += [(f"c{g}{t}", b + o + 4), (f"n{g}{t}", b + o + 11)]
        pe += [("T_x" + g, b + 18)]
        act += [("hi_" + g, b + 19)]
        dve += [("lo_" + g, b + 20)]
    act += [("ev_bv", 97), ("tanh_bv", 99), ("sq_bv", 100), ("ev_bu", 105), ("tanh_bu", 107), ("hi_B", 111)]
    dve += [("poly_bv", 98), ("gelu_bv", 100), ("rs_bv", 102), ("norm_bv", 104),
            ("poly_bu", 106), ("gelu_bu", 108), ("gate_B", 109), ("lo_B", 112)]
    pe += [("z_B", 106), ("T_xB", 110)]
    pe += [("gb_0", 44), ("gb_1", 45)]
    dve += [("g_0", 46), ("g_1", 47)]
    act, dve = ([(name, at + AHEAD) for name, at in s] for s in (act, dve))
    return [sorted(s, key=lambda x: x[1]) for s in (pe, act, dve)]
PE_SIDE, ACT_SIDE, DVE_SIDE = _steps()


def build_trunk(nc, x, c, w_mod, b_mod, w_in, w_out, a_qnorm, a_knorm, a_lambda, a_subln, b_vnorm,
                b_ws, b_bias, c_qnorm, c_knorm, w_ff1, w_ff2, rope, out):
    ctx = ExitStack()

    def sb(name, shape, dt=F32):
        return ctx.enter_context(nc.sbuf_tensor(name, shape, dt))

    def ps(name, shape):
        return ctx.enter_context(nc.psum_tensor(name, shape, F32))

    def sem(name):
        return ctx.enter_context(nc.semaphore(name))

    with ctx:
        x_sb = sb("x_sb", [P, T, D])
        act_hi = sb("act_hi", [P, KT, S], F32R)
        act_lo = sb("act_lo", [P, KT, S], F32R)
        mid_hi = sb("mid_hi", [P, KT, S], F32R)
        mid_lo = sb("mid_lo", [P, KT, S], F32R)
        raw_w = sb("raw_w", [P, RAW_SLOTS, UNIT_KT, N])
        w_hi = sb("w_hi", [P, SPLIT_SLOTS, UNIT_KT, N], F32R)
        w_lo = sb("w_lo", [P, SPLIT_SLOTS, UNIT_KT, N], F32R)
        raw_mod = sb("raw_mod", [P, MOD_SLOTS, MODW])
        mod_acc = sb("mod_acc", [P, 2, MODW])
        gate = sb("gate", [P, D])
        stage = sb("stage", [P, 4, T * N])
        keys = sb("keys", [P, 4, S])
        queries = sb("queries", [P, 4, S])
        values = sb("values", [P, T, N])
        scores = sb("scores", [P, 4, S])
        probs_t = sb("probs_t", [P, 8, P])
        mask = sb("mask", [P, T, S])
        idx_keys = probs_t[:].rearrange("p a b -> p (a b)")[:, 0:2 * S].rearrange("p (a b) -> p a b", a=2)
        square = probs_t[:].rearrange("p a b -> p (a b)")[:, N:2 * N]
        ident = sb("ident", [P, P])
        ones = sb("ones", [P, 1])
        rope_sb = sb("rope_sb", [P, T, 2 * DH + 2 * IDX_DH])
        cos128, sin128 = rope_sb[:, :, 0:DH], rope_sb[:, :, DH:2 * DH]
        cos64 = rope_sb[:, :, 2 * DH:2 * DH + IDX_DH]
        sin64 = rope_sb[:, :, 2 * DH + IDX_DH:2 * DH + 2 * IDX_DH]
        gained = sb("gained", [P, 2, T, DH])
        qk_gain = sb("qk_gain", [P, 4, DH])
        sub_gain = sb("sub_gain", [P, 2 * DH])
        v_gain = sb("v_gain", [P, N])
        ws_raw = values[:].rearrange("p t n -> p (t n)")[:, 0:N].rearrange("p (g j) -> p g j", g=4)
        ws_t = sb("ws_t", [P, 4, P])
        bias_raw = sb("bias_raw", [4, P])
        bias_t = sb("bias_t", [P, 4])
        b_mod_sb = sb("b_mod_sb", [96, DEPTH, P])
        c_rows = sb("c_rows", [KT, P])
        c_raw = sb("c_raw", [P, KT])
        c_exp = sb("c_exp", [P, KT])
        c_act = sb("c_act", [P, KT])
        mod_col = sb("mod_col", [P, 6, KT])
        scale_col = sb("scale_col", [P, KT])
        idx_w = sb("idx_w", [P, T, IDX_HEADS])
        sums = sb("sums", [P, 16])
        rs = sb("rs", [P, 16])
        newton = sb("newton", [P, 3, 16])
        newton_i = newton[:, 1, :].bitcast(I32)
        row_ss = sb("row_ss", [P, T])
        row_r = sb("row_r", [P, T])
        head_ss = sb("head_ss", [P, 2])
        row_max = sb("row_max", [P, 4])
        row_sum = sb("row_sum", [P, T, 4])
        row_inv = sb("row_inv", [P, T, 4])
        top8 = sb("top8", [P, 8])
        lam = sb("lam", [P, 4])
        neg_lam = sb("neg_lam", [P, DEPTH])
        main = [ps(f"main{i}", [P, T, N]) for i in range(2)]
        aux = [ps(f"aux{i}", [P, T * N]) for i in range(2)]

        raw_loaded = [sem(f"raw_loaded{i}") for i in range(RAW_SLOTS)]
        hi_ready, lo_ready, unit_used = sem("hi_ready"), sem("lo_ready"), sem("unit_used")
        mod_loaded = [sem(f"mod_loaded{i}") for i in range(MOD_SLOTS)]
        mod_used, mod_reduced, mod_ready = sem("mod_used"), sem("mod_reduced"), sem("mod_ready")
        main_free_act, main_free_dve = sem("main_free_act"), sem("main_free_dve")
        pe_step = [sem(f"pe_step{l}") for l in range(DEPTH)]
        act_step = [sem(f"act_step{l}") for l in range(DEPTH)]
        dve_step = [sem(f"dve_step{l}") for l in range(DEPTH)]
        act_link, dve_link = sem("act_link"), sem("dve_link")
        norm_ss, norm_r, norm_x = sem("norm_ss"), sem("norm_r"), sem("norm_x")
        norm_t, norm_h, norm_split = sem("norm_t"), sem("norm_h"), sem("norm_split")
        gate_sum, gate2_ready = sem("gate_sum"), sem("gate2_ready")
        hidden_ready, hidden_t = sem("hidden_ready"), sem("hidden_t")
        hidden_hi, hidden_lo = sem("hidden_hi"), sem("hidden_lo")
        gated, x_ready = sem("gated"), sem("x_ready")
        c_loaded, x_loaded, const_loaded = sem("c_loaded"), sem("x_loaded"), sem("const_loaded")
        gains_loaded = [sem(f"gains_loaded{l}") for l in range(DEPTH)]
        lam_loaded, zeroed, ident_ready = sem("lam_loaded"), sem("zeroed"), sem("ident_ready")
        c_t, c_exp_ready, c_ready = sem("c_t"), sem("c_exp_ready"), sem("c_ready")
        lam_dots, lam_exp, lam_ready = sem("lam_dots"), sem("lam_exp"), sem("lam_ready")
        stored = sem("stored")

        def step_value(steps, name):
            return [s for s, _ in steps].index(name) + 1

        def after_pe(eng, l, name):
            eng.wait_ge(pe_step[l], step_value(PE_SIDE, name))

        def after_act(eng, l, name):
            eng.wait_ge(act_step[l], step_value(ACT_SIDE, name))

        def after_dve(eng, l, name):
            eng.wait_ge(dve_step[l], step_value(DVE_SIDE, name))

        def mod_halves(l):
            return {u0 + i: (HALVES_BEFORE[l] + n, p, h, i)
                    for n, (p, h, u0) in enumerate(mod_plan(l)) for i in range(HALF_TILES)}

        def round_tile_at(i):
            return 2 + AHEAD + (i * 15) // 8

        ROUND_TILES = {round_tile_at(i): i for i in range(2 * HALF_TILES)}
        aux_of = {}

        block = ctx.enter_context(nc.Block())

        @block.tensor
        def _(pe):
            held = [None, None]
            taken = [0]

            def take_aux(key, free):
                n = taken[0] % 2
                taken[0] += 1
                if held[n] is not None:
                    pe.wait_ge(*held[n])
                held[n] = free
                aux_of[key] = n
                return aux[n]

            def act_frees(l, name):
                return act_step[l], step_value(ACT_SIDE, name)

            def dve_frees(l, name):
                return dve_step[l], step_value(DVE_SIDE, name)

            def products(slot, left_hi, left_lo, kt0, first, last, bank, width=N):
                for s in range(UNIT_KT):
                    kt = kt0 + s
                    for t in range(T):
                        acc = main[bank][:, t, 0:width]
                        hi = left_hi[:, kt, t * P:(t + 1) * P]
                        lo = left_lo[:, kt, t * P:(t + 1) * P]
                        begin = first and s == 0
                        end = last and s == UNIT_KT - 1
                        nc.tensor.matmul(acc, hi, w_hi[:, slot, s, 0:width], start=begin, stop=False)
                        nc.tensor.matmul(acc, hi, w_lo[:, slot, s, 0:width], start=False, stop=False)
                        ins = nc.tensor.matmul(acc, lo, w_hi[:, slot, s, 0:width], start=False, stop=end)
                ins.then_inc(unit_used, 1)

            def transposes(dst, src):
                for t in range(T):
                    blocks = src(t).rearrange("p (b c) -> p b c", c=P)
                    for b in range(blocks.shape[1]):
                        at = b * S + t * P
                        ins = nc.tensor.transpose(dst[:, at:at + P], blocks[:, b, :], ident[:])
                return ins

            def mod_reduce(half, param, h, done):
                l = 0 if half < HALVES_BEFORE[0] + len(mod_plan(0)) else 1
                dst = take_aux(("mod", half), (mod_ready, half + 1))
                pe.wait_ge(mod_used, done)
                cols = MODW // P
                nc.tensor.matmul(dst[:, 0:cols], b_mod_sb[:, l, :],
                                 ident[0:96, bass.ds(param * KT + h * cols, cols)],
                                 start=True, stop=False)
                for j in range(cols):
                    ins = nc.tensor.matmul(dst[:, j:j + 1], mod_acc[:, h, j * P:(j + 1) * P], ones[:],
                                           start=False, stop=(j == cols - 1))
                ins.then_inc(mod_reduced, 1)

            def gate_rows(param, i, dst):
                for j in range(8):
                    col = mod_col[:, param, 8 * i + j:8 * i + j + 1].to_broadcast([P, P])
                    ins = nc.tensor.matmul(dst[:, j * P:(j + 1) * P], col, ident[:], start=True, stop=True)
                return ins

            def side(l, name):
                done = pe_step[l]
                if name == "T_ws":
                    dst = take_aux((l, name), dve_frees(l, "ws"))
                    pe.wait_ge(gains_loaded[l], 16 * 8)
                    after_dve(pe, l, "ws_mask")
                    for g in range(4):
                        nc.tensor.transpose(dst[:, g * P:(g + 1) * P], ws_raw[:, g, :], ident[:])
                    nc.tensor.transpose(dst[:, N:N + 4], bias_raw[:], ident[0:4, 0:4]).then_inc(done, 1)
                elif name == "T_ik":
                    dst = take_aux((l, name), act_frees(l, "tv_ik"))
                    after_dve(pe, l, "rope_ik")
                    transposes(dst, lambda t: stage[:, 1, t * S:t * S + 2 * P]).then_inc(done, 1)
                elif name.startswith("T_x"):
                    g = name[3:]
                    dst = take_aux((l, name), dve_frees(l, "lo_" + g))
                    if g == "B":
                        after_dve(pe, l, "gate_B")
                    elif g == "C":
                        after_act(pe, l, "vC1")
                    else:
                        after_dve(pe, l, f"n{g}1")
                    buf = 1 if g == "B" else 3
                    transposes(dst, lambda t: stage[:, buf, t * N:(t + 1) * N]).then_inc(done, 1)
                elif name.startswith("T_"):
                    chunk = name[2:]
                    dst = take_aux((l, name), act_frees(l, "tv_" + chunk))
                    after_dve(pe, l, "rope_" + chunk)
                    transposes(dst, lambda t: stage[:, 1, t * N:(t + 1) * N]).then_inc(done, 1)
                elif name.startswith("idx"):
                    i = int(name[3])
                    dst = take_aux((l, name), dve_frees(l, f"isc{i}"))
                    after_act(pe, l, "tv_iq")
                    t, heads = (0, range(8)) if i == 0 else (1, range(4 * i - 4, 4 * i))
                    nk = P * (t + 1)
                    for j, h in enumerate(heads):
                        ins = nc.tensor.matmul(dst[:, j * nk:(j + 1) * nk],
                                               queries[:, h // 2, t * P:(t + 1) * P],
                                               idx_keys[:, h % 2, 0:nk], start=True, stop=True)
                    ins.then_inc(done, 1)
                elif name.startswith("gb_"):
                    i = int(name[3])
                    dst = take_aux((l, name), dve_frees(l, f"g_{i}"))
                    if i == 0:
                        pe.wait_ge(mod_ready, g1_halves(l))
                    gate_rows(G1, i, dst).then_inc(done, 1)
                elif name == "z_B":
                    dst = take_aux((l, name), dve_frees(l, "gate_B"))
                    after_dve(pe, l, "norm_bv")
                    vn = queries[:].rearrange("p a b -> p (a b)")
                    for t in range(T):
                        for g in range(4):
                            at = t * N + g * P
                            ins = nc.tensor.matmul(dst[:, at:at + P], ws_t[:, g, :], vn[:, at:at + P],
                                                   start=True, stop=True)
                    ins.then_inc(done, 1)
                else:
                    kind, g, t = name[0], name[1:-1], int(name[-1])
                    nk = P * (t + 1)
                    if kind == "s":
                        dst = take_aux((l, name), dve_frees(l, f"m{g}{t}"))
                        if t == 0:
                            after_act(pe, l, {"C": "tv_cq", "A0": "tv_aq0", "A1": "tv_aq1"}[g])
                        for m in range(4):
                            ins = nc.tensor.matmul(dst[:, m * nk:(m + 1) * nk],
                                                   queries[:, m, t * P:(t + 1) * P], keys[:, m, 0:nk],
                                                   start=True, stop=True)
                    elif kind == "p":
                        dst = take_aux((l, name), act_frees(l, f"t{g}{t}"))
                        if g == "C":
                            after_act(pe, l, f"e{g}{t}")
                        else:
                            after_dve(pe, l, f"c{g}{t}")
                        heads = [0, 1, 2, 3] if g == "C" else [0, 2]
                        j = 0
                        for h in heads:
                            for k in range(t + 1):
                                ins = nc.tensor.transpose(dst[:, j * P:(j + 1) * P],
                                                          scores[:, h, k * P:(k + 1) * P], ident[:])
                                j += 1
                    else:
                        dst = take_aux((l, name), act_frees(l, f"v{g}{t}"))
                        after_act(pe, l, f"t{g}{t}")
                        if t == 0:
                            after_act(pe, l, {"C": "ev_cv", "A0": "ev_av0", "A1": "ev_av1"}[g])
                        n_heads = 4 if g == "C" else 2
                        dv = N // n_heads
                        for h in range(n_heads):
                            for k in range(t + 1):
                                ins = nc.tensor.matmul(dst[:, h * dv:(h + 1) * dv],
                                                       probs_t[:, h * (t + 1) + k, :],
                                                       values[:, k, h * dv:(h + 1) * dv],
                                                       start=(k == 0), stop=(k == t))
                    ins.then_inc(done, 1)

            def norm(nn):
                for g in range(4):
                    dst = take_aux(("norm", nn, g), (norm_h, 4 * nn + g + 1))
                    pe.wait_ge(norm_x, 4 * nn + g + 1)
                    transposes(dst, lambda t: stage[:, g % 2, t * N:(t + 1) * N]).then_inc(norm_t, 1)

            def ff_round(l, q, base, k_end):
                r0 = l * ROUNDS * UP + UP * q
                for k in range(2, k_end):
                    n = base + k
                    up = k % ROUND_UNITS < UP * UNITS
                    j = k // UNITS
                    pe.wait_ge(lo_ready, n + 1)
                    if k % UNITS == 0:
                        c2 = j - 2
                        if j % 8 in (0, 1, 6, 7):
                            pe.wait_ge(main_free_dve, l * LAYER_DVE_CHUNKS + N_OUT_CHUNKS + UP * q
                                       + (j - 2 - UP if j >= 6 else j - 2) + 1)
                        else:
                            pe.wait_ge(main_free_act, l * LAYER_ACT_CHUNKS + N_IN_CHUNKS + UP * q + c2 + 1)
                    if not up and k % UNITS in (0, 2, 4, 6) and j == UP:
                        pe.wait_ge(hidden_lo, r0 + (k % UNITS) // 2 + 1)
                    left = (act_hi, act_lo) if up else (mid_hi, mid_lo)
                    products(k % SPLIT_SLOTS, left[0], left[1], UNIT_KT * (k % UNITS), k % UNITS == 0,
                             k % UNITS == UNITS - 1, (l * LAYER_CHUNKS + N_IN_CHUNKS + N_OUT_CHUNKS + j) % 2)
                    if k % UNITS == 1 and 1 <= j <= UP:
                        i = j - 1
                        if l == 0:
                            free = (mod_ready, round_half(q) - 1 + i) if i < 2 else (hidden_lo, r0 + i - 1)
                        else:
                            free = (hidden_lo, r0 + i - 1)
                        pe.wait_ge(*free)
                        pe.wait_ge(hidden_ready, r0 + i + 1)
                        transposes(aux[(aux0 + i) % 2],
                                   lambda t: stage[:, 0, t * N:(t + 1) * N]).then_inc(hidden_t, 1)
                    if l == 0 and k == 34:
                        round_reduce(q, 0, r0)
                    if l == 0 and k == 62:
                        round_reduce(q, 1, r0)

            def round_half(q):
                return HALVES_BEFORE[0] + len(mod_plan(0)) + 2 * q

            def round_reduce(q, h, r0):
                pe.wait_ge(hidden_lo, r0 + 3 + h)
                pe.wait_ge(mod_used, HALF_TILES * (round_half(q) + h + 1))
                dst, cols = aux[(aux0 + h) % 2], MODW // P
                nc.tensor.matmul(dst[:, 0:cols], b_mod_sb[:, 1, :],
                                 ident[0:96, bass.ds(q * KT + h * cols, cols)], start=True, stop=False)
                for j in range(cols):
                    ins = nc.tensor.matmul(dst[:, j:j + 1], mod_acc[:, h, j * P:(j + 1) * P], ones[:],
                                           start=False, stop=(j == cols - 1))
                ins.then_inc(mod_reduced, 1)

            def g1_halves(l):
                return HALVES_BEFORE[0] + 2 if l == 0 else HALVES_BEFORE[0] + len(mod_plan(0)) + 6

            pe.wait_ge(ident_ready, 2)
            pe.wait_ge(c_loaded, 16)
            dst = take_aux("c", (c_ready, 1))
            nc.tensor.transpose(dst[:, 0:KT], c_rows[:], ident[0:KT, 0:KT]).then_inc(c_t, 1)
            pe.wait_ge(const_loaded, 32)
            pe.wait_ge(zeroed, 1)
            for half in range(HALVES_BEFORE[0]):
                mod_reduce(half, half // 2, half % 2, HALF_TILES * (half + 1))
            for l in range(DEPTH):
                norm(2 * l)
                plan = mod_halves(l)
                steps = list(PE_SIDE)
                for k in range(STRAIGHT_UNITS):
                    n = l * LAYER_UNITS + k
                    pe.wait_ge(lo_ready, n + 1)
                    if k < IN_UNITS:
                        j, u = divmod(k, UNITS)
                        if u % 2 == 0 and j == 0:
                            pe.wait_ge(norm_split, 4 * 2 * l + u // 2 + 1)
                        left, kt0, first, last = (act_hi, act_lo), UNIT_KT * u, u == 0, u == UNITS - 1
                        width = IN_CHUNKS[IN_NAMES[j]][1]
                        if first:
                            if j >= 2:
                                pe.wait_ge(main_free_act, l * LAYER_ACT_CHUNKS + j - 1)
                            elif l:
                                pe.wait_ge(main_free_dve, l * LAYER_DVE_CHUNKS - 1 + j)
                    else:
                        (j, kt0, first, last), width = OUT_UNITS[k - IN_UNITS], N
                        left = (mid_hi, mid_lo)
                        if first:
                            if j >= 2:
                                pe.wait_ge(main_free_dve, l * LAYER_DVE_CHUNKS + j - 1)
                            else:
                                pe.wait_ge(main_free_act, l * LAYER_ACT_CHUNKS + N_IN_CHUNKS - 1 + j)
                        group = {KT_C: "C", KT_A0: "A0", KT_B: "B", KT_A1: "A1"}.get(kt0)
                        if group and j == 0:
                            after_dve(pe, l, "lo_" + group)
                        j += N_IN_CHUNKS
                    products(k % SPLIT_SLOTS, left[0], left[1], kt0, first, last,
                             (l * LAYER_CHUNKS + j) % 2, width)
                    while steps and steps[0][1] <= k:
                        side(l, steps.pop(0)[0])
                    if k - 1 in plan and plan[k - 1][3] == HALF_TILES - 1:
                        half, p, h, _ = plan[k - 1]
                        mod_reduce(half, p, h, HALF_TILES * (half + 1))
                assert not steps
                if STRAIGHT_UNITS - 1 in plan:
                    half, p, h, _ = plan[STRAIGHT_UNITS - 1]
                    mod_reduce(half, p, h, HALF_TILES * (half + 1))
                norm(2 * l + 1)
                base = l * LAYER_UNITS + STRAIGHT_UNITS
                for k in (0, 1):
                    pe.wait_ge(lo_ready, base + k + 1)
                    if k == 0:
                        pe.wait_ge(norm_split, 4 * (2 * l + 1) + 1)
                        pe.wait_ge(main_free_dve, l * LAYER_DVE_CHUNKS + N_OUT_CHUNKS - 1)
                    products(k, act_hi, act_lo, UNIT_KT * k, k == 0, False,
                             (l * LAYER_CHUNKS + N_IN_CHUNKS + N_OUT_CHUNKS) % 2)
                for i in (0, 1):
                    dst = take_aux(("gb2", l, i), (gate2_ready, 2 * l + i + 1))
                    if i == 0:
                        pe.wait_ge(mod_ready, HALVES_BEFORE[l] + len(mod_plan(l)))
                    gate_rows(G2, i, dst).then_inc(gate_sum, 1)
                pe.wait_ge(norm_split, 4 * (2 * l + 2))
                for n in (0, 1):
                    pe.wait_ge(*held[n])
                aux0 = taken[0] % 2
                aux_of["rounds", l] = aux0
                with pe.Fori(0, ROUNDS - 1) as q:
                    ff_round(l, q, base + ROUND_UNITS * q, ROUND_UNITS + 2)
                q = ROUNDS - 1
                ff_round(l, q, base + ROUND_UNITS * q, ROUND_UNITS)
                held[aux0] = (mod_ready, round_half(q) + 1) if l == 0 else (hidden_lo, (l + 1) * ROUNDS * UP - 1)
                held[1 - aux0] = (mod_ready, round_half(q) + 2) if l == 0 else (hidden_lo, (l + 1) * ROUNDS * UP)

        @block.scalar
        def _(act):
            links = [0]

            def link(ins):
                links[0] += 1
                ins.then_inc(act_link, 1)
                act.wait_ge(act_link, links[0])

            def round_hi(n, n_over_slots, slot, half, width=N):
                act.wait_ge(raw_loaded[slot], 16 * (n_over_slots + 1))
                if not isinstance(n, int) or n >= SPLIT_SLOTS:
                    act.wait_ge(unit_used, n - SPLIT_SLOTS + 1)
                nc.scalar.activation(w_hi[:, half, :, 0:width], raw_w[:, slot, :, 0:width],
                                     ACT.Copy).then_inc(hi_ready, 1)

            def hi(n):
                k = n % LAYER_UNITS
                width = IN_CHUNKS[IN_NAMES[k // UNITS]][1] if k < IN_UNITS else N
                round_hi(n, n // RAW_SLOTS, n % RAW_SLOTS, n % SPLIT_SLOTS, width)

            def side(l, name):
                done = act_step[l]
                kind, _, what = name.partition("_")
                if step_value(ACT_SIDE, name) > 1:
                    act.wait_ge(done, step_value(ACT_SIDE, name) - 1)
                if kind == "ev":
                    c = IN_NAMES.index(what)
                    bank, width = main[(l * LAYER_CHUNKS + c) % 2], IN_CHUNKS[what][1]
                    act.wait_ge(unit_used, l * LAYER_UNITS + UNITS * (c + 1))
                    if what in ("cv", "av0", "av1"):
                        if what != "cv":
                            after_pe(act, l, {"av0": "oC1", "av1": "oA01"}[what])
                        nc.scalar.activation(values[:], bank[:], ACT.Copy).then_inc(main_free_act, 1)
                        act.wait_ge(main_free_act, l * LAYER_ACT_CHUNKS + c + 1)
                        act.sem_inc(done, 1)
                        return
                    raw = stage[:, 0, :].rearrange("p (t n) -> p t n", t=T)
                    if what == "ik":
                        act.wait_ge(norm_t, 4 * (2 * l + 1))
                    else:
                        after_dve(act, l, prev_reader(what))
                        if what in ROPED or what == "bv":
                            after_pe(act, l, "T_" + prev_transposed(what))
                    nc.scalar.activation(raw[:, :, 0:width], bank[:, :, 0:width],
                                         ACT.Copy).then_inc(main_free_act, 1)
                    act.wait_ge(main_free_act, l * LAYER_ACT_CHUNKS + c + 1)
                    if what in ("ik", "iq"):
                        act.sem_inc(done, 1)
                    else:
                        nc.scalar.activation(stage[:, 1, :], stage[:, 0, :], ACT.Square).then_inc(done, 1)
                elif kind == "tv":
                    after_pe(act, l, "T_" + what)
                    src = aux[aux_of[l, "T_" + what]][:]
                    if what == "ik":
                        dst, src = idx_keys[:], src[:, 0:2 * S]
                    elif what in ("ck", "ak0", "ak1"):
                        if what != "ck":
                            after_pe(act, l, {"ak0": "sC1", "ak1": "sA01"}[what])
                        dst = keys[:]
                    else:
                        if what != "iq":
                            after_pe(act, l, {"cq": "idx2", "aq0": "sC1", "aq1": "sA01"}[what])
                        dst = queries[:]
                    nc.scalar.activation(dst.rearrange("p a b -> p (a b)"), src, ACT.Copy).then_inc(done, 1)
                elif kind == "tanh":
                    after_dve(act, l, "poly_" + what)
                    nc.scalar.activation(stage[:, 2, :], stage[:, 1, :], ACT.Tanh,
                                         scale=GELU_B).then_inc(done, 1)
                elif kind == "sq":
                    after_dve(act, l, "gelu_bv")
                    nc.scalar.activation(stage[:, 1, :], stage[:, 2, :], ACT.Square).then_inc(done, 1)
                elif kind == "hi":
                    g = what
                    after_pe(act, l, "T_x" + g)
                    kt = {"C": KT_C, "A0": KT_A0, "B": KT_B, "A1": KT_A1}[g]
                    nc.scalar.activation(mid_hi[:, kt:kt + 4, :].rearrange("p a b -> p (a b)"),
                                         aux[aux_of[l, "T_x" + g]][:], ACT.Copy).then_inc(done, 1)
                else:
                    kind, g, t = name[0], name[1:-1], int(name[-1])
                    nk = P * (t + 1)
                    if kind == "e":
                        after_dve(act, l, f"m{g}{t}")
                        for m in range(4):
                            ins = nc.scalar.activation(scores[:, m, 0:nk], scores[:, m, 0:nk], ACT.Exp,
                                                       bias=row_max[:, m:m + 1],
                                                       accum_out=row_sum[:, t, m:m + 1])
                        ins.then_inc(done, 1)
                    elif kind == "t":
                        after_pe(act, l, f"p{g}{t}")
                        if t == 1:
                            after_pe(act, l, f"o{g}0")
                        elif g != "C":
                            after_pe(act, l, {"A0": "oC1", "A1": "oA01"}[g])
                        n = (4 if g == "C" else 2) * (t + 1)
                        nc.scalar.activation(probs_t[:, 0:n, :].rearrange("p a b -> p (a b)"),
                                             aux[aux_of[l, f"p{g}{t}"]][:, 0:n * P],
                                             ACT.Copy).then_inc(done, 1)
                    else:
                        after_pe(act, l, f"o{g}{t}")
                        src = aux[aux_of[l, f"o{g}{t}"]]
                        if t == 0 and g != "C":
                            after_pe(act, l, {"A0": "T_xC", "A1": "T_xA0"}[g])
                        if g == "C":
                            after_dve(act, l, f"i{g}{t}")
                            for h in range(4):
                                ins = nc.scalar.activation(
                                    stage[:, 3, t * N + h * DH:t * N + (h + 1) * DH],
                                    src[:, h * DH:(h + 1) * DH], ACT.Copy, scale=row_inv[:, t, h:h + 1])
                        else:
                            if not (g == "A0" and t == 0):
                                after_dve(act, l, "nA00" if g == "A0" else ("nA01" if t == 0 else "nA10"))
                            nc.scalar.activation(stage[:, 3, t * N:(t + 1) * N], src[:, 0:N], ACT.Copy)
                            for h in range(2):
                                ins = nc.scalar.activation(square[:, h * 2 * DH:(h + 1) * 2 * DH],
                                                           src[:, h * 2 * DH:(h + 1) * 2 * DH], ACT.Square,
                                                           accum_out=head_ss[:, h:h + 1])
                        ins.then_inc(done, 1)

            def norm(nn, x_count):
                l, second = divmod(nn, 2)
                if x_count:
                    act.wait_ge(x_ready, x_count)
                else:
                    act.wait_ge(x_loaded, 16 * T)
                    act.wait_ge(lam_dots, 1)
                for t in range(T):
                    junk = stage[:, 2 * t:2 * t + 2, :].rearrange("p a b -> p (a b)")
                    ins = nc.scalar.activation(junk, x_sb[:, t, :], ACT.Square, accum_out=row_ss[:, t:t + 1])
                ins.then_inc(norm_ss, 1)
                act.wait_ge(norm_r, nn + 1)
                shift = SH2 if second else SH1

                def rows(g):
                    if g >= 2:
                        act.wait_ge(norm_t, 4 * nn + g - 1)
                    for t in range(T):
                        ins = nc.scalar.activation(stage[:, g % 2, t * N:(t + 1) * N],
                                                   x_sb[:, t, g * N:(g + 1) * N], ACT.Copy,
                                                   scale=row_r[:, t:t + 1])
                    ins.then_inc(norm_x, 1)

                def modulate(g):
                    act.wait_ge(norm_t, 4 * nn + g + 1)
                    if g >= 2:
                        act.wait_ge(norm_split, 4 * nn + g - 1)
                    src = aux[aux_of["norm", nn, g]]
                    for j in range(4):
                        kt = 4 * g + j
                        ins = nc.scalar.activation(stage[:, 2 + g % 2, j * S:(j + 1) * S],
                                                   src[:, j * S:(j + 1) * S], ACT.Identity,
                                                   bias=mod_col[:, shift, kt:kt + 1],
                                                   scale=scale_col[:, kt:kt + 1])
                    ins.then_inc(norm_h, 1)

                rows(0)
                rows(1)
                modulate(0)
                rows(2)
                modulate(1)
                rows(3)
                modulate(2)
                modulate(3)

            def ff_round(l, q, base, k_end):
                r0 = l * ROUNDS * UP + UP * q
                for k in range(2 + AHEAD, k_end):
                    round_hi(base + k, (l * LAYER_UNITS + STRAIGHT_UNITS) // RAW_SLOTS
                             + (ROUND_UNITS // RAW_SLOTS) * q + k // RAW_SLOTS,
                             k % RAW_SLOTS, k % SPLIT_SLOTS)
                    j, u = divmod(k, UNITS)
                    if u == 1 + AHEAD and 1 <= j <= UP:
                        i = j - 1
                        bank = main[(l * LAYER_CHUNKS + N_IN_CHUNKS + N_OUT_CHUNKS + i) % 2]
                        act.wait_ge(unit_used, base + UNITS * j)
                        nc.scalar.activation(stage[:, 0, :], bank[:].rearrange("p t n -> p (t n)"),
                                             ACT.Relu).then_inc(main_free_act, 1)
                        act.wait_ge(main_free_act,
                                    l * LAYER_ACT_CHUNKS + N_IN_CHUNKS + UP * q + i + 1)
                        nc.scalar.activation(stage[:, 0, :], stage[:, 0, :],
                                             ACT.Square).then_inc(hidden_ready, 1)
                    if u == 3 + AHEAD and 1 <= j <= UP:
                        i = j - 1
                        act.wait_ge(hidden_t, r0 + i + 1)
                        nc.scalar.activation(mid_hi[:, 4 * i:4 * i + 4, :].rearrange("p a b -> p (a b)"),
                                             aux[(aux_of["rounds", l] + i) % 2][:],
                                             ACT.Copy).then_inc(hidden_hi, 1)

            def prev_reader(what):
                order = ["ik", "iq", "ck", "cq", "ak0", "aq0", "ak1", "aq1", "bv", "bu"]
                before = order[order.index(what) - 1]
                return {"bv": "norm_bv"}.get(before, "rope_" + before)

            def prev_transposed(what):
                order = ["ik", "iq", "ck", "cq", "ak0", "aq0", "ak1", "aq1", "bv"]
                return order[order.index(what) - 1]

            act.wait_ge(c_t, 1)
            nc.scalar.activation(c_exp[:], aux[aux_of["c"]][:, 0:KT], ACT.Exp,
                                 scale=-1.0).then_inc(c_exp_ready, 1)
            act.wait_ge(lam_dots, 1)
            nc.scalar.activation(lam[:], lam[:], ACT.Exp).then_inc(lam_exp, 1)
            for l in range(DEPTH):
                first = l * LAYER_UNITS
                for k in range(2 + AHEAD):
                    hi(first + k)
                norm(2 * l, l * LAYER_DVE_CHUNKS)
                steps = list(ACT_SIDE)
                for k in range(2 + AHEAD, STRAIGHT_UNITS + 2 + AHEAD):
                    hi(first + k)
                    while steps and steps[0][1] <= k:
                        side(l, steps.pop(0)[0])
                assert not steps
                norm(2 * l + 1, l * LAYER_DVE_CHUNKS + N_OUT_CHUNKS)
                base = first + STRAIGHT_UNITS
                with act.Fori(0, ROUNDS - 1) as q:
                    ff_round(l, q, base + ROUND_UNITS * q, ROUND_UNITS + 2 + AHEAD)
                q = ROUNDS - 1
                ff_round(l, q, base + ROUND_UNITS * q, ROUND_UNITS)

        @block.vector
        def _(dve):
            links = [0]
            V = nc.vector

            def link(ins):
                links[0] += 1
                ins.then_inc(dve_link, 1)
                dve.wait_ge(dve_link, links[0])

            def lo(n, slot, half, width=N):
                dve.wait_ge(hi_ready, n + 1)
                V.tensor_tensor(w_lo[:, half, :, 0:width], raw_w[:, slot, :, 0:width],
                                w_hi[:, half, :, 0:width].bitcast(F32), ALU.subtract).then_inc(lo_ready, 1)

            def straight_lo(n):
                k = n % LAYER_UNITS
                width = IN_CHUNKS[IN_NAMES[k // UNITS]][1] if k < IN_UNITS else N
                lo(n, n % RAW_SLOTS, n % SPLIT_SLOTS, width)

            def mod_tile(half, h, kt, over_slots):
                m = HALF_TILES * half + kt
                slot = kt % MOD_SLOTS
                dve.wait_ge(mod_loaded[slot], 16 * (over_slots + 1))
                acc, tile = mod_acc[:, h, :], raw_mod[:, slot, :]
                if kt == 0:
                    if not isinstance(half, int) or half >= 2:
                        dve.wait_ge(mod_reduced, half - 1)
                    V.tensor_scalar(acc, tile, c_act[:, 0:1], None, ALU.mult).then_inc(mod_used, 1)
                else:
                    dve.wait_ge(mod_used, m)
                    V.scalar_tensor_tensor(out=acc, in0=tile, scalar=c_act[:, kt:kt + 1], in1=acc,
                                           op0=ALU.mult, op1=ALU.add).then_inc(mod_used, 1)

            def mod_columns(half, param, h, src):
                dve.wait_ge(mod_reduced, half + 1)
                at = param * KT + h * (MODW // P)
                cols = mod_col[:].rearrange("p a b -> p (a b)")
                V.tensor_copy(cols[:, bass.ds(at, MODW // P)], src[:, 0:MODW // P]).then_inc(mod_ready, 1)

            def rsqrt(out, ss, inv_n, n):
                v, g, w = newton[:, 0, 0:n], newton[:, 1, 0:n], newton[:, 2, 0:n]
                bits = newton_i[:, 0:n]
                link(V.tensor_scalar(v, ss, inv_n, EPS, ALU.mult, ALU.add))
                link(V.tensor_scalar(bits, v.bitcast(I32), 1, None, ALU.logical_shift_right))
                link(V.tensor_scalar(bits, bits, -1.0, float(0x5F3759DF), ALU.mult, ALU.add))
                for i in range(3):
                    link(V.tensor_tensor(w, g, g, ALU.mult))
                    link(V.scalar_tensor_tensor(out=w, in0=w, scalar=-0.5, in1=v, op0=ALU.mult, op1=ALU.mult))
                    last = V.scalar_tensor_tensor(out=out if i == 2 else g, in0=w, scalar=1.5, in1=g,
                                                  op0=ALU.add, op1=ALU.mult)
                    if i < 2:
                        link(last)
                return last

            def heads(i, n_heads, dh, c0=0, c1=None):
                v = stage[:, i, :].rearrange("p (t h d) -> p t h d", t=T, h=n_heads)
                return v[:, :, :, c0:dh if c1 is None else c1]

            def over_heads(table, n_heads):
                shape = list(table.shape)
                return table.unsqueeze(2).broadcast_to([P, shape[1], n_heads, shape[2]])

            def side(l, name):
                done = dve_step[l]
                kind, _, what = name.partition("_")
                if step_value(DVE_SIDE, name) > 1:
                    dve.wait_ge(done, step_value(DVE_SIDE, name) - 1)
                if name == "ws_mask":
                    dve.wait_ge(gains_loaded[l], 16 * 8)
                    V.memset(ws_raw[0:CHUNK, :, CHUNK:P], 0.0)
                    V.tensor_scalar(sub_gain[:], sub_gain[:], 1.0 - (0.8 - 0.6 * math.exp(-0.3 * l)), None,
                                    ALU.mult).then_inc(done, 1)
                elif name == "ws":
                    after_pe(dve, l, "T_ws")
                    src = aux[aux_of[l, "T_ws"]]
                    V.tensor_copy(ws_t[:].rearrange("p a b -> p (a b)"), src[:, 0:N])
                    V.tensor_copy(bias_t[:], src[:, N:N + 4]).then_inc(done, 1)
                elif name == "rope_ik":
                    after_act(dve, l, "ev_ik")
                    raw = stage[:, 0, :].rearrange("p (t n) -> p t n", t=T)
                    work = stage[:, 2, :].rearrange("p (t n) -> p t n", t=T)
                    half = IDX_DH // 2
                    link(V.memset(stage[:, 1, 0:2 * S], 0.0))
                    V.tensor_scalar(idx_w[:], raw[:, :, IDX_DH:IDX_DH + IDX_HEADS], IDX_SCALE, None, ALU.mult)
                    V.tensor_tensor(work[:, :, 0:IDX_DH], raw[:, :, 0:IDX_DH], cos64, ALU.mult)
                    V.tensor_tensor(work[:, :, IDX_DH:IDX_DH + half], raw[:, :, half:IDX_DH],
                                    sin64[:, :, 0:half], ALU.mult)
                    link(V.tensor_tensor(work[:, :, IDX_DH + half:2 * IDX_DH], raw[:, :, 0:half],
                                         sin64[:, :, half:IDX_DH], ALU.mult))
                    pair = stage[:, 1, 0:2 * S].rearrange("p (t n) -> p t n", t=T)
                    for at in (0, P + IDX_DH):
                        ins = V.tensor_tensor(pair[:, :, at:at + IDX_DH], work[:, :, 0:IDX_DH],
                                              work[:, :, IDX_DH:2 * IDX_DH], ALU.add)
                    ins.then_inc(done, 1)
                elif name == "rope_iq":
                    after_act(dve, l, "ev_iq")
                    after_pe(dve, l, "T_ik")
                    half, nh = IDX_DH // 2, IDX_HEADS
                    V.tensor_tensor(heads(1, nh, IDX_DH), heads(0, nh, IDX_DH), over_heads(cos64, nh), ALU.mult)
                    V.tensor_tensor(heads(2, nh, IDX_DH, 0, half), heads(0, nh, IDX_DH, half),
                                    over_heads(sin64[:, :, 0:half], nh), ALU.mult)
                    link(V.tensor_tensor(heads(2, nh, IDX_DH, half), heads(0, nh, IDX_DH, 0, half),
                                         over_heads(sin64[:, :, half:], nh), ALU.mult))
                    V.tensor_tensor(stage[:, 1, :], stage[:, 1, :], stage[:, 2, :], ALU.add).then_inc(done, 1)
                elif kind == "rs" and what != "bv":
                    after_act(dve, l, "ev_" + what)
                    link(V.tensor_reduce(sums[:, 0:8], stage[:, 1, :].rearrange("p (a b) -> p a b", b=DH),
                                         AX.X, ALU.add))
                    rsqrt(rs[:, 0:8], sums[:, 0:8], 1.0 / DH, 8).then_inc(done, 1)
                elif kind == "mul":
                    gain = qk_gain[:, {"aq": 0, "ak": 1, "cq": 2, "ck": 3}[what[:2]], :]
                    half = DH // 2

                    def over_t(x):
                        return x.unsqueeze(1).broadcast_to([P, T, x.shape[1]])
                    V.tensor_tensor(gained[:, 0, :, :], cos128, over_t(gain), ALU.mult)
                    V.tensor_tensor(gained[:, 1, :, 0:half], sin128[:, :, 0:half], over_t(gain[:, half:]), ALU.mult)
                    link(V.tensor_tensor(gained[:, 1, :, half:], sin128[:, :, half:], over_t(gain[:, 0:half]),
                                         ALU.mult))
                    V.tensor_tensor(heads(1, 4, DH), heads(0, 4, DH), over_heads(gained[:, 0, :, :], 4),
                                    ALU.mult).then_inc(done, 1)
                elif kind == "rope":
                    half = DH // 2
                    V.tensor_tensor(heads(2, 4, DH, 0, half), heads(0, 4, DH, half),
                                    over_heads(gained[:, 1, :, 0:half], 4), ALU.mult)
                    link(V.tensor_tensor(heads(2, 4, DH, half), heads(0, 4, DH, 0, half),
                                         over_heads(gained[:, 1, :, half:], 4), ALU.mult))
                    link(V.tensor_tensor(stage[:, 1, :], stage[:, 1, :], stage[:, 2, :], ALU.add))
                    flat = stage[:, 1, :].rearrange("p (a b) -> p a b", b=DH)
                    V.tensor_tensor(flat, flat, rs[:, 0:8].unsqueeze(2).broadcast_to([P, 8, DH]),
                                    ALU.mult).then_inc(done, 1)
                elif kind[:3] == "isc":
                    i = int(name[3])
                    after_pe(dve, l, f"idx{i}")
                    t = 0 if i == 0 else 1
                    nh, nk, h0 = (8, P, 0) if i == 0 else (4, S, 4 * i - 4)
                    work = scores[:].rearrange("p a b -> p (a b)").rearrange("p (h k) -> p h k", h=nh)
                    src = aux[aux_of[l, f"idx{i}"]][:].rearrange("p (h k) -> p h k", h=nh)
                    link(V.scalar_tensor_tensor(out=work, in0=src, scalar=0.0,
                                                in1=idx_w[:, t, h0:h0 + nh].unsqueeze(2).broadcast_to([P, nh, nk]),
                                                op0=ALU.max, op1=ALU.mult))
                    dst = mask[:, t, 0:nk] if i < 2 else gained[:].rearrange("p a b c -> p (a b c)")[:, 0:nk]
                    red = V.tensor_reduce(dst, work.rearrange("p h k -> p k h"), AX.X, ALU.add)
                    if i == 2:
                        link(red)
                        red = V.tensor_tensor(mask[:, 1, :], mask[:, 1, :], dst, ALU.add)
                    red.then_inc(done, 1)
                elif kind[:4] == "topk":
                    t = int(name[4])
                    nk = P * (t + 1)
                    dve.wait_ge(done, step_value(DVE_SIDE, f"isc{2 * t}"))
                    link(V.memset(mask[0:CHUNK, t, nk - CHUNK:nk], NEG))
                    src = mask[:, t, 0:nk]
                    for r in range(TOPK // 8):
                        dst = scores[:, 2 * t + r % 2, 0:nk]
                        link(V.max(top8[:], src))
                        rep = V.match_replace(dst, top8[:], src, TAKEN)
                        if r < TOPK // 8 - 1:
                            link(rep)
                        src = dst
                    rep.then_inc(done, 1)
                elif name == "mask":
                    dve.wait_ge(done, step_value(DVE_SIDE, "topk1"))
                    for t in range(T):
                        nk = P * (t + 1)
                        left = scores[:, 2 * t + 1, 0:nk]
                        link(V.tensor_scalar(left, left, TAKEN, None, ALU.is_equal))
                        link(V.scalar_tensor_tensor(out=left, in0=mask[:, t, 0:nk], scalar=0.5 * NEG, in1=left,
                                                    op0=ALU.is_gt, op1=ALU.mult))
                        ins = V.tensor_scalar(mask[:, t, 0:nk], left, -1.0, -NEG, ALU.add, ALU.mult)
                        if t == 0:
                            link(ins)
                    ins.then_inc(done, 1)
                elif name == "maskA":
                    link(V.memset(mask[:], 0.0))
                    V.memset(mask[0:CHUNK, 0, CHUNK:P], NEG)
                    V.memset(mask[0:CHUNK, 1, S - CHUNK:S], NEG).then_inc(done, 1)
                elif kind == "g":
                    i = int(what)
                    after_pe(dve, l, f"gb_{i}")
                    V.tensor_copy(gate[:, i * 1024:(i + 1) * 1024],
                                  aux[aux_of[l, f"gb_{i}"]][:]).then_inc(done, 1)
                elif kind == "poly":
                    after_act(dve, l, "ev_" + what)
                    link(V.tensor_scalar(stage[:, 1, :], stage[:, 1, :], GELU_A, 1.0, ALU.mult, ALU.add))
                    V.tensor_tensor(stage[:, 1, :], stage[:, 1, :], stage[:, 0, :], ALU.mult).then_inc(done, 1)
                elif kind == "gelu":
                    after_act(dve, l, "tanh_" + what)
                    link(V.scalar_tensor_tensor(out=stage[:, 2, :], in0=stage[:, 2, :], scalar=1.0,
                                                in1=stage[:, 0, :], op0=ALU.add, op1=ALU.mult))
                    V.tensor_scalar(stage[:, 2, :], stage[:, 2, :], 0.5, None, ALU.mult).then_inc(done, 1)
                elif name == "rs_bv":
                    after_act(dve, l, "sq_bv")
                    link(V.tensor_reduce(sums[:, 0:8], stage[:, 1, :].rearrange("p (a b) -> p a b", b=P),
                                         AX.X, ALU.add))
                    link(rsqrt(rs[:, 0:8], sums[:, 0:8], 1.0 / P, 8))
                    flat = stage[:, 2, :].rearrange("p (a b) -> p a b", b=P)
                    V.tensor_tensor(flat, flat, rs[:, 0:8].unsqueeze(2).broadcast_to([P, 8, P]),
                                    ALU.mult).then_inc(done, 1)
                elif name == "norm_bv":
                    dve.wait_ge(done, step_value(DVE_SIDE, "rs_bv"))
                    after_pe(dve, l, "sA11")
                    V.tensor_tensor(queries[:].rearrange("p a b -> p (a b)").rearrange("p (t n) -> p t n", t=T),
                                    stage[:, 2, :].rearrange("p (t n) -> p t n", t=T),
                                    v_gain[:].unsqueeze(1).broadcast_to([P, T, N]), ALU.mult).then_inc(done, 1)
                elif name == "gate_B":
                    after_pe(dve, l, "z_B")
                    dve.wait_ge(done, step_value(DVE_SIDE, "gelu_bu"))
                    z = aux[aux_of[l, "z_B"]][:].rearrange("p (t g c) -> p t g c", t=T, g=4)
                    for g in range(4):
                        ins = V.scalar_tensor_tensor(out=heads(1, 4, P)[:, :, g, :], in0=z[:, :, g, :],
                                                     scalar=bias_t[:, g:g + 1], in1=heads(2, 4, P)[:, :, g, :],
                                                     op0=ALU.add, op1=ALU.mult)
                    ins.then_inc(done, 1)
                elif kind == "lo":
                    g = what
                    after_act(dve, l, "hi_" + g)
                    kt = {"C": KT_C, "A0": KT_A0, "B": KT_B, "A1": KT_A1}[g]
                    V.tensor_tensor(mid_lo[:, kt:kt + 4, :].rearrange("p a b -> p (a b)"),
                                    aux[aux_of[l, "T_x" + g]][:],
                                    mid_hi[:, kt:kt + 4, :].bitcast(F32).rearrange("p a b -> p (a b)"),
                                    ALU.subtract).then_inc(done, 1)
                else:
                    kind, g, t = name[0], name[1:-1], int(name[-1])
                    nk = P * (t + 1)
                    if kind == "m":
                        after_pe(dve, l, f"s{g}{t}")
                        if t == 1:
                            after_pe(dve, l, f"p{g}0")
                        elif g != "C":
                            after_pe(dve, l, {"A0": "pC1", "A1": "pA01"}[g])
                        src = aux[aux_of[l, f"s{g}{t}"]][:, 0:4 * nk].rearrange("p (m k) -> p m k", m=4)
                        link(V.scalar_tensor_tensor(out=scores[:, :, 0:nk], in0=src, scalar=QK_SCALE,
                                                    in1=mask[:, t, 0:nk].unsqueeze(1).broadcast_to([P, 4, nk]),
                                                    op0=ALU.mult, op1=ALU.add))
                        V.tensor_reduce(row_max[:], scores[:, :, 0:nk], AX.X, ALU.max,
                                        negate=True).then_inc(done, 1)
                    elif kind == "i":
                        after_act(dve, l, f"e{g}{t}")
                        V.reciprocal(row_inv[:, t, :], row_sum[:, t, :]).then_inc(done, 1)
                    elif kind == "c":
                        after_act(dve, l, f"e{g}{t}")
                        link(V.reciprocal(row_inv[:, t, :], row_sum[:, t, :]))
                        odd = row_inv[:, t, :].rearrange("p (h m) -> p h m", m=2)[:, :, 1]
                        link(V.tensor_scalar(odd, odd, neg_lam[:, l:l + 1], None, ALU.mult))
                        for m in (0, 2):
                            link(V.tensor_scalar(scores[:, m, 0:nk], scores[:, m, 0:nk],
                                                 row_inv[:, t, m:m + 1], None, ALU.mult))
                            ins = V.scalar_tensor_tensor(out=scores[:, m, 0:nk], in0=scores[:, m + 1, 0:nk],
                                                         scalar=row_inv[:, t, m + 1:m + 2],
                                                         in1=scores[:, m, 0:nk], op0=ALU.mult, op1=ALU.add)
                        ins.then_inc(done, 1)
                    else:
                        after_act(dve, l, f"v{g}{t}")
                        link(rsqrt(rs[:, 8:10], head_ss[:], 1.0 / (2 * DH), 2))
                        for h in range(2):
                            at = t * N + h * 2 * DH
                            ins = V.scalar_tensor_tensor(out=stage[:, 3, at:at + 2 * DH],
                                                         in0=stage[:, 3, at:at + 2 * DH],
                                                         scalar=rs[:, 8 + h:9 + h], in1=sub_gain[:],
                                                         op0=ALU.mult, op1=ALU.mult)
                        ins.then_inc(done, 1)

            def norm(nn):
                l, second = divmod(nn, 2)
                V.tensor_scalar(scale_col[:], mod_col[:, SC2 if second else SC1, :], 1.0, None, ALU.add)
                dve.wait_ge(norm_ss, nn + 1)
                rsqrt(row_r[:], row_ss[:], 1.0 / D, T).then_inc(norm_r, 1)

            def split(nn):
                for g in range(4):
                    dve.wait_ge(norm_h, 4 * nn + g + 1)
                    rows = stage[:, 2 + g % 2, :].rearrange("p (a b) -> p a b", a=4)
                    kts = slice(4 * g, 4 * g + 4)
                    link(V.tensor_copy(act_hi[:, kts, :], rows))
                    V.tensor_tensor(act_lo[:, kts, :], rows, act_hi[:, kts, :].bitcast(F32),
                                    ALU.subtract).then_inc(norm_split, 1)

            def gate_chunk(bank, j, used, before):
                dve.wait_ge(unit_used, used)
                if before is not None:
                    dve.wait_ge(x_ready, before)
                V.tensor_tensor(stage[:, 2, :].rearrange("p (t n) -> p t n", t=T), main[bank][:],
                                gate[:, j * N:(j + 1) * N].unsqueeze(1).broadcast_to([P, T, N]),
                                ALU.mult).then_inc(main_free_dve, 1)

            def add_chunk(j, count):
                cols = slice(j * N, (j + 1) * N)
                dve.wait_ge(main_free_dve, count)
                V.tensor_tensor(x_sb[:, :, cols], x_sb[:, :, cols],
                                stage[:, 2, :].rearrange("p (t n) -> p t n", t=T), ALU.add).then_inc(x_ready, 1)

            def ff_round(l, q, base, k_end):
                r0 = l * ROUNDS * UP + UP * q
                for k in range(2 + AHEAD, k_end):
                    lo(base + k, k % RAW_SLOTS, k % SPLIT_SLOTS)
                    j, u = divmod(k, UNITS)
                    if l == 0 and k in ROUND_TILES:
                        h, kt = divmod(ROUND_TILES[k], HALF_TILES)
                        half = round_half(q) + h
                        mod_tile(half, h, kt, (HALF_TILES // MOD_SLOTS) * half + kt // MOD_SLOTS)
                    if u == 4 + AHEAD and 1 <= j <= UP:
                        i = j - 1
                        dve.wait_ge(hidden_hi, r0 + i + 1)
                        V.tensor_tensor(mid_lo[:, 4 * i:4 * i + 4, :].rearrange("p a b -> p (a b)"),
                                        aux[(aux_of["rounds", l] + i) % 2][:],
                                        mid_hi[:, 4 * i:4 * i + 4, :].bitcast(F32).rearrange("p a b -> p (a b)"),
                                        ALU.subtract).then_inc(hidden_lo, 1)
                    if l == 0 and k in (36 + AHEAD, 64 + AHEAD - 1):
                        round_columns(l, q, 0 if k == 36 + AHEAD else 1)
                    if u == 1 + AHEAD and j > UP:
                        gate_down(l, q, base, j - 1)
                    if j > UP and u == (2 + AHEAD if j < 2 * UP else 1 + AHEAD):
                        add_down(l, q, j - 1)
                if k_end == ROUND_UNITS:
                    if l == 0:
                        round_columns(l, q, 1)
                    gate_down(l, q, base, 2 * UP - 1)
                    add_down(l, q, 2 * UP - 1)

            def round_half(q):
                return HALVES_BEFORE[0] + len(mod_plan(0)) + 2 * q

            def round_columns(l, q, h):
                mod_columns(round_half(q) + h, q, h, aux[(aux_of["rounds", l] + h) % 2])

            def down_count(l, q, j):
                return l * LAYER_DVE_CHUNKS + N_OUT_CHUNKS + UP * q + j - UP

            def gate_down(l, q, base, j):
                gate_chunk((l * LAYER_CHUNKS + N_IN_CHUNKS + N_OUT_CHUNKS + j) % 2, j - UP,
                           base + UNITS * (j + 1), down_count(l, q, j))

            def add_down(l, q, j):
                add_chunk(j - UP, down_count(l, q, j) + 1)

            dve.wait_ge(lam_loaded, 16)
            prod = stage[:, 2, 0:DEPTH * 2 * DH].rearrange("p (a b) -> p a b", b=DH)
            both = stage[:, 1, 0:DEPTH * 4 * DH].rearrange("p (a m b) -> p a m b", m=2, b=DH)
            link(V.tensor_tensor(prod, both[:, :, 0, :], both[:, :, 1, :], ALU.mult))
            V.tensor_reduce(lam[:], prod, AX.X, ALU.add).then_inc(lam_dots, 1)
            dve.wait_ge(c_exp_ready, 1)
            link(V.tensor_copy(c_raw[:], aux[aux_of["c"]][:, 0:KT]))
            link(V.tensor_scalar(c_exp[:], c_exp[:], 1.0, None, ALU.add))
            link(V.reciprocal(c_exp[:], c_exp[:]))
            V.tensor_tensor(c_act[:], c_raw[:], c_exp[:], ALU.mult).then_inc(c_ready, 1)
            dve.wait_ge(c_ready, 1)
            dve.wait_ge(lam_exp, 1)
            for l in range(DEPTH):
                link(V.tensor_tensor(neg_lam[:, l:l + 1], lam[:, 2 * l + 1:2 * l + 2], lam[:, 2 * l:2 * l + 1],
                                     ALU.subtract))
                link(V.tensor_scalar(neg_lam[:, l:l + 1], neg_lam[:, l:l + 1],
                                     -(0.8 - 0.6 * math.exp(-0.3 * l)), None, ALU.add))
            for half in range(HALVES_BEFORE[0]):
                for kt in range(HALF_TILES):
                    mod_tile(half, half % 2, kt, (HALF_TILES * half + kt) // MOD_SLOTS)
                if half:
                    mod_columns(half - 1, (half - 1) // 2, (half - 1) % 2, aux[aux_of["mod", half - 1]])
            half = HALVES_BEFORE[0] - 1
            mod_columns(half, half // 2, half % 2, aux[aux_of["mod", half]])
            for l in range(DEPTH):
                first = l * LAYER_UNITS
                for k in range(2 + AHEAD):
                    straight_lo(first + k)
                dve.wait_ge(mod_ready, HALVES_BEFORE[l])
                norm(2 * l)
                split(2 * l)
                plan = mod_halves(l)
                steps = list(DVE_SIDE)
                finished = {IN_UNITS + i + 2 + AHEAD: OUT_UNITS[i][0] for i in range(N_OUT_CHUNKS * UNITS)
                            if OUT_UNITS[i][3]}
                for k in range(2 + AHEAD, STRAIGHT_UNITS + 2 + AHEAD):
                    straight_lo(first + k)
                    if k in plan:
                        half, p, h, kt = plan[k]
                        mod_tile(half, h, kt, (HALF_TILES * half + kt) // MOD_SLOTS)
                    if k - 3 - AHEAD in plan and plan[k - 3 - AHEAD][3] == HALF_TILES - 1:
                        half, p, h, _ = plan[k - 3 - AHEAD]
                        mod_columns(half, p, h, aux[aux_of["mod", half]])
                    if k in finished:
                        j = finished[k]
                        count = l * LAYER_DVE_CHUNKS + j
                        gate_chunk((l * LAYER_CHUNKS + N_IN_CHUNKS + j) % 2, j, first + k - 1 - AHEAD,
                                   count or None)
                        add_chunk(j, count + 1)
                    while steps and steps[0][1] <= k:
                        side(l, steps.pop(0)[0])
                assert not steps
                if STRAIGHT_UNITS - 1 in plan:
                    half, p, h, _ = plan[STRAIGHT_UNITS - 1]
                    mod_columns(half, p, h, aux[aux_of["mod", half]])
                dve.wait_ge(mod_ready, HALVES_BEFORE[l] + len(mod_plan(l)))
                norm(2 * l + 1)
                split(2 * l + 1)
                for i in (0, 1):
                    dve.wait_ge(gate_sum, 2 * l + i + 1)
                    V.tensor_copy(gate[:, i * 1024:(i + 1) * 1024],
                                  aux[aux_of["gb2", l, i]][:]).then_inc(gate2_ready, 1)
                base = first + STRAIGHT_UNITS
                with dve.Fori(0, ROUNDS - 1) as q:
                    ff_round(l, q, base + ROUND_UNITS * q, ROUND_UNITS + 2 + AHEAD)
                q = ROUNDS - 1
                ff_round(l, q, base + ROUND_UNITS * q, ROUND_UNITS)

        @block.gpsimd
        def _(pool):
            nc.gpsimd.memset(ident[:], 0.0).then_inc(ident_ready, 1)
            nc.gpsimd.memset(ones[:], 1.0).then_inc(zeroed, 1)
            pool.wait_ge(ident_ready, 1)
            nc.gpsimd.affine_select(out=ident[:], in_=ident[:], compare_op=ALU.not_equal, fill=1.0, base=0,
                                    pattern=[[-1, P]], channel_multiplier=1).then_inc(ident_ready, 1)

        @block.sync
        def _(sp):
            def load_unit(n, slot, src):
                if not isinstance(n, int) or n >= RAW_SLOTS:
                    sp.wait_ge(lo_ready, n - RAW_SLOTS + 1)
                width = src.shape[-1]
                sp.dma_start(raw_w[:, slot, :, 0:width],
                             src.rearrange("(s p) n -> p s n", p=P)).then_inc(raw_loaded[slot], 16)

            def load_mod(l, half, param, h, kt):
                m, slot = HALF_TILES * half + kt, kt % MOD_SLOTS
                if not isinstance(m, int) or m >= MOD_SLOTS:
                    sp.wait_ge(mod_used, m - MOD_SLOTS + 1)
                sp.dma_start(raw_mod[:, slot, :], w_mod[l, kt * P:(kt + 1) * P, bass.ds(param * D + h * MODW, MODW)]
                             ).then_inc(mod_loaded[slot], 16)

            sp.dma_start(c_rows[:], c[0, :].rearrange("(a b) -> a b", b=P)).then_inc(c_loaded, 16)
            sp.dma_start(stage[:, 1, 0:DEPTH * 4 * DH],
                         a_lambda.rearrange("l m d -> (l m d)").partition_broadcast(P)).then_inc(lam_loaded, 16)
            sp.dma_start(b_mod_sb[:], b_mod.rearrange("l (r c) -> r l c", c=P)).then_inc(const_loaded, 16)
            sp.dma_start(rope_sb[:], rope.rearrange("(t p) n -> p t n", p=P)).then_inc(const_loaded, 16)
            for t in range(T):
                sp.dma_start(x_sb[:, t, :], x[0, t * P:(t + 1) * P, :]).then_inc(x_loaded, 16)
            for half in range(HALVES_BEFORE[0]):
                for kt in range(HALF_TILES):
                    load_mod(0, half, half // 2, half % 2, kt)
            for l in range(DEPTH):
                if l:
                    after_pe(sp, l - 1, PE_SIDE[-1][0])
                    after_act(sp, l - 1, ACT_SIDE[-1][0])
                    after_dve(sp, l - 1, DVE_SIDE[-1][0])
                loaded = gains_loaded[l]
                for i, gain in enumerate((a_qnorm, a_knorm, c_qnorm, c_knorm)):
                    sp.dma_start(qk_gain[:, i, :], gain[l, :].partition_broadcast(P)).then_inc(loaded, 16)
                sp.dma_start(sub_gain[:], a_subln[l, :].partition_broadcast(P)).then_inc(loaded, 16)
                sp.dma_start(v_gain[:], b_vnorm[l, :].partition_broadcast(P)).then_inc(loaded, 16)
                sp.dma_start(ws_raw[:], b_ws[l].rearrange("g i j -> i g j")).then_inc(loaded, 16)
                sp.dma_start(bias_raw[:], b_bias[l]).then_inc(loaded, 16)
                plan = mod_halves(l)
                for k in range(STRAIGHT_UNITS):
                    n = l * LAYER_UNITS + k
                    if k < IN_UNITS:
                        j, u = divmod(k, UNITS)
                        col, width = IN_CHUNKS[IN_NAMES[j]]
                        src = w_in[l, UNIT_KT * P * u:UNIT_KT * P * (u + 1), col:col + width]
                    else:
                        j, kt0, _, _ = OUT_UNITS[k - IN_UNITS]
                        src = w_out[l, kt0 * P:(kt0 + UNIT_KT) * P, j * N:(j + 1) * N]
                    load_unit(n, n % RAW_SLOTS, src)
                    if k in plan:
                        load_mod(l, *plan[k])
                base = l * LAYER_UNITS + STRAIGHT_UNITS
                with sp.Fori(0, ROUNDS) as q:
                    for k in range(ROUND_UNITS):
                        j, u = divmod(k, UNITS)
                        if j < UP:
                            src = w_ff1[l, UNIT_KT * P * u:UNIT_KT * P * (u + 1), bass.ds(q * D + j * N, N)]
                        else:
                            src = w_ff2[l, bass.ds(q * D + UNIT_KT * P * u, UNIT_KT * P),
                                        (j - UP) * N:(j - UP + 1) * N]
                        load_unit(base + ROUND_UNITS * q + k, k % RAW_SLOTS, src)
                        if l == 0 and k in ROUND_TILES:
                            h, kt = divmod(ROUND_TILES[k], HALF_TILES)
                            load_mod(1, HALVES_BEFORE[0] + len(mod_plan(0)) + 2 * q + h, q, h, kt)
            for j in range(D // N):
                sp.wait_ge(x_ready, DEPTH * LAYER_DVE_CHUNKS - UP + j + 1)
                for t in range(T):
                    sp.dma_start(out[0, t * P:(t + 1) * P, j * N:(j + 1) * N],
                                 x_sb[:, t, j * N:(j + 1) * N]).then_inc(stored, 16)
            sp.wait_ge(stored, 16 * T * (D // N))


_INS = ["x", "c", "w_mod", "b_mod", "w_in", "w_out", "a_qnorm", "a_knorm", "a_lambda", "a_subln", "b_vnorm",
        "b_ws", "b_bias", "c_qnorm", "c_knorm", "w_ff1", "w_ff2"]


def rope_table():
    parts = []
    for dim in (DH, IDX_DH):
        inv = np.float32(1.0) / (np.float32(10000.0) ** (np.arange(0, dim, 2, dtype=np.float32) / np.float32(dim)))
        ang = np.arange(S, dtype=np.float32)[:, None] * inv[None, :].astype(np.float32)
        cos, sin = np.cos(ang), np.sin(ang)
        parts += [cos, cos, -sin, sin]
    return np.ascontiguousarray(np.concatenate(parts, axis=1), dtype=np.float32)


def kernel(**inputs):
    import concourse.bacc as bacc
    from concourse.bass_utils import run_bass_kernel_spmd

    nc = bacc.Bacc("TRN2", target_bir_lowering=False, num_devices=1, dynamic_dma_scratch_size=1024)
    arrays = {f"in_{n}_dram": np.ascontiguousarray(inputs[n]) for n in _INS}
    arrays["in_rope_dram"] = rope_table()
    args = [nc.dram_tensor(n, a.shape, mybir.dt.from_np(a.dtype), kind="ExternalInput").ap()
            for n, a in arrays.items()]
    args.append(nc.dram_tensor("out_dram", (1, S, D), F32, kind="ExternalOutput").ap())
    build_trunk(nc, *args)
    r = run_bass_kernel_spmd(nc, [arrays], core_ids=[0])
    return r.results[0]["out_dram"]
```

```python
import math
from contextlib import ExitStack

import numpy as np

import concourse.bass as bass
from concourse import mybir

F32 = mybir.dt.float32
F32R = mybir.dt.float32r
I32 = mybir.dt.int32
ACT = mybir.ActivationFunctionType
ALU = mybir.AluOpType
AX = mybir.AxisListType

P = 128
D = 2048
S = 256
T = S // P
KT = D // P
DEPTH = 2
D_FF = 4 * D
CHUNK = 64
EPS = 1e-6
NEG = -1e30
TAKEN = -3e38
TOPK = S // 4
DH = 128
IDX_HEADS, IDX_DH = 8, 64
N = 512
UNIT_KT = 2
UNITS = KT // UNIT_KT
RAW_SLOTS, SLOTS, MOD_SLOTS = 8, 4, 2
AHEAD = 2
MOD_BEHIND = 2
MODW = 1024
HALF_TILES = KT
QK_SCALE = DH ** -0.5
IDX_SCALE = IDX_HEADS ** -0.5 * IDX_DH ** -0.5
GELU_A, GELU_B = 0.044715, math.sqrt(2.0 / math.pi)

IN_CHUNKS = {
    "ik": (6144, 72), "iq": (5632, N), "ck": (4608, N), "cq": (4096, N), "cv": (5120, N),
    "ak0": (1024, N), "aq0": (0, N), "av0": (2048, N),
    "ak1": (1536, N), "aq1": (512, N), "av1": (2560, N), "bv": (3584, N), "bu": (3072, N),
}
IN_NAMES = list(IN_CHUNKS)
N_IN_CHUNKS = len(IN_NAMES)
N_OUT_CHUNKS = D // N
UP = D // N
ROUNDS = D_FF // D
IN_UNITS = N_IN_CHUNKS * UNITS
STRAIGHT_UNITS = IN_UNITS + N_OUT_CHUNKS * UNITS
ROUND_UNITS = 2 * UP * UNITS
LAYER_UNITS = STRAIGHT_UNITS + ROUNDS * ROUND_UNITS
LAYER_CHUNKS = LAYER_UNITS // UNITS
LAYER_ACT_CHUNKS = N_IN_CHUNKS + ROUNDS * UP
LAYER_DVE_CHUNKS = N_OUT_CHUNKS + ROUNDS * UP

KT_C, KT_A0, KT_B, KT_A1 = 12, 0, 8, 4
def _out_units():
    early = [KT_C, KT_C + 2, KT_A0, KT_A0 + 2]
    late = [KT_B, KT_B + 2, KT_A1, KT_A1 + 2]
    units = []
    for part in (early, late):
        for j in (0, 1):
            units += [(j, k, part is early and k == early[0], part is late and k == late[-1]) for k in part]
    for j in (2, 3):
        units += [(j, k, k == early[0], k == late[-1]) for k in early + late]
    return units
OUT_UNITS = _out_units()

SH1, SC1, G1, SH2, SC2, G2 = range(6)
def mod_plan(l):
    params = [G1, SH2, SC2] if l == 0 else [SC2, G2]
    tiles = 2 * len(params) * HALF_TILES
    units = [UNITS + (i * (STRAIGHT_UNITS - UNITS - 2)) // tiles for i in range(tiles)]
    return [(p, h, units[(2 * i + h) * HALF_TILES:(2 * i + h + 1) * HALF_TILES])
            for i, p in enumerate(params) for h in (0, 1)]
FIRST_HALVES = 4
ROUND0_HALF = FIRST_HALVES + len(mod_plan(0))
HALVES_BEFORE = [FIRST_HALVES, ROUND0_HALF + 4 + 2 * (ROUNDS - 1)]

ROPED = ["ck", "cq", "ak0", "aq0", "ak1", "aq1"]
def evac_at(name):
    return IN_NAMES.index(name) * UNITS + UNITS + 1
GROUPS = {"C": 47, "A0": 67, "A1": 90}

CHUNK_AT = dict(rs=0, mul=1, rope=3, sc=5, T=6, tv=7)
TILE_AT = dict(s=0, m=2, e=4, i=3, c=4, p=6, t=7, o=8, v=9, n=10)
TILE_GAP = 4
MIX_AT = dict(T=17, hi=18, lo=18)
SOLO_AT = dict(
    T_ws=6, ws_mask=3, ws=8, T_ik=12, T_iq=22, idx0=24, idx1=27, idx2=30, ev_ik=9, tv_ik=12, ev_iq=17,
    tv_iq=24, rope_ik=9, rope_iq=18, isc0=25, isc1=29, isc2=33, topk0=40, topk1=44, mask=45, maskA=64,
    ev_bv=97, tanh_bv=99, sq_bv=100, ev_bu=105, tanh_bu=108, hi_B=111, poly_bv=98, gelu_bv=100, rs_bv=102,
    norm_bv=104, poly_bu=106, gelu_bu=106, gate_B=109, lo_B=112, z_B=106, T_xB=110, gb_0=89, gb_1=89, g_0=90,
    g_1=90)


def _steps():
    engines = {"pe": "T_ws T_ik T_iq idx0 idx1 idx2 z_B T_xB gb_0 gb_1",
               "act": "ev_ik tv_ik ev_iq tv_iq ev_bv tanh_bv sq_bv ev_bu tanh_bu hi_B"}
    engines = {e: names.split() for e, names in engines.items()}
    pe, act = ([(s, SOLO_AT[s]) for s in engines[e]] for e in ("pe", "act"))
    dve = [(s, at) for s, at in SOLO_AT.items() if s not in engines["pe"] + engines["act"]]
    for c in ROPED:
        e = evac_at(c)
        act += [("ev_" + c, e), ("sc_" + c, e + CHUNK_AT["sc"]), ("tv_" + c, e + CHUNK_AT["tv"])]
        dve += [(f"{s}_{c}", e + CHUNK_AT[s]) for s in ("rs", "mul", "rope")]
        pe += [("T_" + c, e + CHUNK_AT["T"])]
    for c in ("cv", "av0", "av1"):
        act += [("ev_" + c, evac_at(c))]
    for g, b in GROUPS.items():
        for t in range(T):
            at = {s: b + TILE_GAP * t + o for s, o in TILE_AT.items()}
            pe += [(f"{s}{g}{t}", at[s]) for s in "spo"]
            act += [(f"{s}{g}{t}", at[s]) for s in "etv"]
            dve += [(f"{s}{g}{t}", at[s]) for s in ("mi" if g == "C" else "mcn")]
        pe += [("T_x" + g, b + MIX_AT["T"])]
        act += [("hi_" + g, b + MIX_AT["hi"])]
        dve += [("lo_" + g, b + MIX_AT["lo"])]
    act, dve = ([(name, at + AHEAD) for name, at in s] for s in (act, dve))
    return [sorted(s, key=lambda x: x[1]) for s in (pe, act, dve)]
PE_SIDE, ACT_SIDE, DVE_SIDE = _steps()


def build_trunk(nc, x, c, w_mod, b_mod, w_in, w_out, a_qnorm, a_knorm, a_lambda, a_subln, b_vnorm,
                b_ws, b_bias, c_qnorm, c_knorm, w_ff1, w_ff2, rope, out):
    ctx = ExitStack()

    def sb(name, shape, dt=F32):
        return ctx.enter_context(nc.sbuf_tensor(name, shape, dt))

    def ps(name, shape):
        return ctx.enter_context(nc.psum_tensor(name, shape, F32))

    def sem(name):
        return ctx.enter_context(nc.semaphore(name))

    with ctx:
        x_sb = sb("x_sb", [P, T, D])
        act_hi = sb("act_hi", [P, KT, S], F32R)
        act_lo = sb("act_lo", [P, KT, S], F32R)
        mid_hi = sb("mid_hi", [P, KT, S], F32R)
        mid_lo = sb("mid_lo", [P, KT, S], F32R)
        w_hi = sb("w_hi", [P, SLOTS, UNIT_KT, N], F32R)
        w_lo = sb("w_lo", [P, SLOTS, UNIT_KT, N], F32R)
        raw_w = sb("raw_w", [P, RAW_SLOTS, UNIT_KT, N])
        raw_mod = sb("raw_mod", [P, MOD_SLOTS, MODW])
        mod_acc = sb("mod_acc", [P, 2, MODW])
        gate = sb("gate", [P, D])
        stage = sb("stage", [P, 4, T * N])
        keys = sb("keys", [P, 4, S])
        queries = sb("queries", [P, 4, S])
        values = sb("values", [P, T, N])
        scores = sb("scores", [P, 4, S])
        probs_t = sb("probs_t", [P, 8, P])
        mask = sb("mask", [P, T, S])
        idx_keys = probs_t[:].rearrange("p a b -> p (a b)")[:, 0:2 * S].rearrange("p (a b) -> p a b", a=2)
        square = probs_t[:].rearrange("p a b -> p (a b)")[:, N:2 * N]
        ident = sb("ident", [P, P])
        ones = sb("ones", [P, 1])
        rope_sb = sb("rope_sb", [P, T, 2 * DH + 2 * IDX_DH])
        cos128, sin128 = rope_sb[:, :, 0:DH], rope_sb[:, :, DH:2 * DH]
        cos64 = rope_sb[:, :, 2 * DH:2 * DH + IDX_DH]
        sin64 = rope_sb[:, :, 2 * DH + IDX_DH:2 * DH + 2 * IDX_DH]
        gained = sb("gained", [P, 2, T, DH])
        r_diag = gained[:, 0, :, :]
        qk_gain = sb("qk_gain", [P, 4, DH])
        sub_gain = sb("sub_gain", [P, 2 * DH])
        v_gain = sb("v_gain", [P, N])
        ws_raw = values[:].rearrange("p t n -> p (t n)")[:, 0:N].rearrange("p (g j) -> p g j", g=4)
        ws_t = sb("ws_t", [P, 4, P])
        bias_raw = sb("bias_raw", [4, P])
        bias_t = sb("bias_t", [P, 4])
        b_mod_sb = sb("b_mod_sb", [96, DEPTH, P])
        c_rows = sb("c_rows", [KT, P])
        c_raw = sb("c_raw", [P, KT])
        c_exp = sb("c_exp", [P, KT])
        c_act = sb("c_act", [P, KT])
        mod_col = sb("mod_col", [P, 6, KT])
        scale_col = sb("scale_col", [P, KT])
        idx_w = sb("idx_w", [P, T, IDX_HEADS])
        sums = sb("sums", [P, 16])
        rs = sb("rs", [P, 16])
        newton = sb("newton", [P, 3, 16])
        newton_i = newton[:, 1, :].bitcast(I32)
        row_parts = sb("row_parts", [P, D // N, T])
        row_ss = sb("row_ss", [P, T])
        row_r = sb("row_r", [P, T])
        head_ss = sb("head_ss", [P, 2])
        row_max = sb("row_max", [P, 4])
        row_sum = sb("row_sum", [P, T, 4])
        row_inv = sb("row_inv", [P, T, 4])
        top8 = sb("top8", [P, 8])
        lam = sb("lam", [P, 4])
        neg_lam = sb("neg_lam", [P, DEPTH])
        main = [ps(f"main{i}", [P, T, N]) for i in range(2)]
        aux = [ps(f"aux{i}", [P, T * N]) for i in range(2)]

        raw_loaded = [sem(f"raw_loaded{i}") for i in range(RAW_SLOTS)]
        hi_ready, lo_ready, unit_used = sem("hi_ready"), sem("lo_ready"), sem("unit_used")
        mod_loaded = [sem(f"mod_loaded{i}") for i in range(MOD_SLOTS)]
        mod_used, mod_reduced, mod_ready = sem("mod_used"), sem("mod_reduced"), sem("mod_ready")
        main_free_act, main_free_dve = sem("main_free_act"), sem("main_free_dve")
        pe_step = [sem(f"pe_step{l}") for l in range(DEPTH)]
        act_step = [sem(f"act_step{l}") for l in range(DEPTH)]
        dve_step = [sem(f"dve_step{l}") for l in range(DEPTH)]
        act_link, dve_link = sem("act_link"), sem("dve_link")
        norm_ss, norm_r, norm_scale = sem("norm_ss"), sem("norm_r"), sem("norm_scale")
        norm_t, norm_h, norm_split = sem("norm_t"), sem("norm_h"), sem("norm_split")
        gate_sum, gate2_ready = sem("gate_sum"), sem("gate2_ready")
        hidden_ready, hidden_t = sem("hidden_ready"), sem("hidden_t")
        hidden_hi, hidden_lo = sem("hidden_hi"), sem("hidden_lo")
        gated, x_ready = sem("gated"), sem("x_ready")
        c_loaded, x_loaded, const_loaded = sem("c_loaded"), sem("x_loaded"), sem("const_loaded")
        gains_loaded = [sem(f"gains_loaded{l}") for l in range(DEPTH)]
        lam_loaded, zeroed, ident_ready = sem("lam_loaded"), sem("zeroed"), sem("ident_ready")
        c_t, c_exp_ready, c_ready = sem("c_t"), sem("c_exp_ready"), sem("c_ready")
        lam_dots, lam_exp, lam_ready = sem("lam_dots"), sem("lam_exp"), sem("lam_ready")
        stored = sem("stored")

        def step_value(steps, name):
            return [s for s, _ in steps].index(name) + 1

        def after_pe(eng, l, name):
            eng.wait_ge(pe_step[l], step_value(PE_SIDE, name))

        def after_act(eng, l, name):
            eng.wait_ge(act_step[l], step_value(ACT_SIDE, name))

        def after_dve(eng, l, name):
            eng.wait_ge(dve_step[l], step_value(DVE_SIDE, name))

        def mod_halves(l):
            return {units[i]: (HALVES_BEFORE[l] + n, p, h, i)
                    for n, (p, h, units) in enumerate(mod_plan(l)) for i in range(HALF_TILES)}

        def round_half(q):
            return ROUND0_HALF if isinstance(q, int) and q == 0 else ROUND0_HALF + 2 + 2 * q

        FIRST_LOADS = HALF_TILES * FIRST_HALVES // RAW_SLOTS

        def mod_slot(half, kt):
            return kt % MOD_SLOTS, (HALF_TILES // MOD_SLOTS) * (half - FIRST_HALVES) + kt // MOD_SLOTS

        def units_beside(nn, g):
            before = 2 if nn == 0 else 2 + AHEAD
            if g < 0:
                return range(before)
            per = -(-(SLOTS - before) // 4)
            return range(min(before + per * g, SLOTS), min(before + per * (g + 1), SLOTS))

        def round_tiles(l, q, k):
            if l > 0:
                return []
            first = isinstance(q, int) and q == 0
            n = (4 if first else 2) * HALF_TILES
            found = [i for i in range(n) if SLOTS + (i * (ROUND_UNITS - 6)) // n == k]
            halves = [(i // HALF_TILES, i % HALF_TILES) for i in found]
            if first:
                return [(h // 2, round_half(q) + h, (G2, SH1)[h // 2], h % 2, i) for h, i in halves]
            return [(1, round_half(q) + h, q, h, i) for h, i in halves]
        finished = {IN_UNITS + i + 2 + AHEAD: unit[0] for i, unit in enumerate(OUT_UNITS) if unit[3]}
        aux_of = {}

        block = ctx.enter_context(nc.Block())

        @block.tensor
        def _(pe):
            held = [None, None]
            taken = [0]

            def take_aux(key, free):
                n = taken[0] % 2
                taken[0] += 1
                if held[n] is not None:
                    pe.wait_ge(*held[n])
                held[n] = free
                aux_of[key] = n
                return aux[n]

            def act_frees(l, name):
                return act_step[l], step_value(ACT_SIDE, name)

            def dve_frees(l, name):
                return dve_step[l], step_value(DVE_SIDE, name)

            def products(slot, left_hi, left_lo, kt0, first, last, bank, width=N):
                for s in range(UNIT_KT):
                    kt = kt0 + s
                    for t in range(T):
                        acc = main[bank][:, t, 0:width]
                        hi = left_hi[:, kt, t * P:(t + 1) * P]
                        lo = left_lo[:, kt, t * P:(t + 1) * P]
                        begin = first and s == 0
                        end = last and s == UNIT_KT - 1
                        nc.tensor.matmul(acc, hi, w_hi[:, slot, s, 0:width], start=begin, stop=False)
                        nc.tensor.matmul(acc, hi, w_lo[:, slot, s, 0:width], start=False, stop=False)
                        ins = nc.tensor.matmul(acc, lo, w_hi[:, slot, s, 0:width], start=False, stop=end)
                ins.then_inc(unit_used, 1)

            def transposes(dst, src):
                for t in range(T):
                    blocks = src(t).rearrange("p (b c) -> p b c", c=P)
                    for b in range(blocks.shape[1]):
                        at = b * S + t * P
                        ins = nc.tensor.transpose(dst[:, at:at + P], blocks[:, b, :], ident[:])
                return ins

            def mod_reduce(half, param, h, l):
                reduce_into(take_aux(("mod", half), (mod_ready, half + 1)), half, param, h, l)

            def reduce_into(dst, half, param, h, l):
                pe.wait_ge(mod_used, HALF_TILES * (half + 1))
                cols = MODW // P
                nc.tensor.matmul(dst[:, 0:cols], b_mod_sb[:, l, :],
                                 ident[0:96, bass.ds(param * KT + h * cols, cols)],
                                 start=True, stop=False)
                for j in range(cols):
                    ins = nc.tensor.matmul(dst[:, j:j + 1], mod_acc[:, h, j * P:(j + 1) * P], ones[:],
                                           start=False, stop=(j == cols - 1))
                ins.then_inc(mod_reduced, 1)

            def gate_rows(param, i, dst):
                for j in range(8):
                    col = mod_col[:, param, 8 * i + j:8 * i + j + 1].to_broadcast([P, P])
                    ins = nc.tensor.matmul(dst[:, j * P:(j + 1) * P], col, ident[:], start=True, stop=True)
                return ins

            def side(l, name):
                done = pe_step[l]
                if name == "T_ws":
                    dst = take_aux((l, name), dve_frees(l, "ws"))
                    pe.wait_ge(gains_loaded[l], 16 * 8)
                    after_dve(pe, l, "ws_mask")
                    for g in range(4):
                        nc.tensor.transpose(dst[:, g * P:(g + 1) * P], ws_raw[:, g, :], ident[:])
                    nc.tensor.transpose(dst[:, N:N + 4], bias_raw[:], ident[0:4, 0:4]).then_inc(done, 1)
                elif name == "T_ik":
                    dst = take_aux((l, name), act_frees(l, "tv_ik"))
                    after_dve(pe, l, "rope_ik")
                    transposes(dst, lambda t: stage[:, 1, t * S:t * S + 2 * P]).then_inc(done, 1)
                elif name.startswith("T_x"):
                    g = name[3:]
                    dst = take_aux((l, name), dve_frees(l, "lo_" + g))
                    if g == "B":
                        after_dve(pe, l, "gate_B")
                    elif g == "C":
                        after_act(pe, l, "vC1")
                    else:
                        after_dve(pe, l, f"n{g}1")
                    buf = 1 if g == "B" else 3
                    transposes(dst, lambda t: stage[:, buf, t * N:(t + 1) * N]).then_inc(done, 1)
                elif name.startswith("T_"):
                    chunk = name[2:]
                    dst = take_aux((l, name), act_frees(l, "tv_" + chunk))
                    if chunk == "iq":
                        after_dve(pe, l, "rope_iq")
                    else:
                        after_act(pe, l, "sc_" + chunk)
                    transposes(dst, lambda t: stage[:, 1, t * N:(t + 1) * N]).then_inc(done, 1)
                elif name.startswith("idx"):
                    i = int(name[3])
                    dst = take_aux((l, name), dve_frees(l, f"isc{i}"))
                    after_act(pe, l, "tv_iq")
                    t, heads = (0, range(8)) if i == 0 else (1, range(4 * i - 4, 4 * i))
                    nk = P * (t + 1)
                    for j, h in enumerate(heads):
                        ins = nc.tensor.matmul(dst[:, j * nk:(j + 1) * nk],
                                               queries[:, h // 2, t * P:(t + 1) * P],
                                               idx_keys[:, h % 2, 0:nk], start=True, stop=True)
                    ins.then_inc(done, 1)
                elif name.startswith("gb_"):
                    i = int(name[3])
                    dst = take_aux((l, name), dve_frees(l, f"g_{i}"))
                    if i == 0:
                        pe.wait_ge(mod_ready, g1_halves(l))
                    gate_rows(G1, i, dst).then_inc(done, 1)
                elif name == "z_B":
                    dst = take_aux((l, name), dve_frees(l, "gate_B"))
                    after_dve(pe, l, "norm_bv")
                    vn = queries[:].rearrange("p a b -> p (a b)")
                    for t in range(T):
                        for g in range(4):
                            at = t * N + g * P
                            ins = nc.tensor.matmul(dst[:, at:at + P], ws_t[:, g, :], vn[:, at:at + P],
                                                   start=True, stop=True)
                    ins.then_inc(done, 1)
                else:
                    kind, g, t = name[0], name[1:-1], int(name[-1])
                    nk = P * (t + 1)
                    if kind == "s":
                        dst = take_aux((l, name), dve_frees(l, f"m{g}{t}"))
                        if t == 0:
                            after_act(pe, l, {"C": "tv_cq", "A0": "tv_aq0", "A1": "tv_aq1"}[g])
                        for m in range(4):
                            ins = nc.tensor.matmul(dst[:, m * nk:(m + 1) * nk],
                                                   queries[:, m, t * P:(t + 1) * P], keys[:, m, 0:nk],
                                                   start=True, stop=True)
                    elif kind == "p":
                        dst = take_aux((l, name), act_frees(l, f"t{g}{t}"))
                        if g == "C":
                            after_act(pe, l, f"e{g}{t}")
                        else:
                            after_dve(pe, l, f"c{g}{t}")
                        heads = [0, 1, 2, 3] if g == "C" else [0, 2]
                        j = 0
                        for h in heads:
                            for k in range(t + 1):
                                ins = nc.tensor.transpose(dst[:, j * P:(j + 1) * P],
                                                          scores[:, h, k * P:(k + 1) * P], ident[:])
                                j += 1
                    else:
                        dst = take_aux((l, name), act_frees(l, f"v{g}{t}"))
                        after_act(pe, l, f"t{g}{t}")
                        if t == 0:
                            after_act(pe, l, {"C": "ev_cv", "A0": "ev_av0", "A1": "ev_av1"}[g])
                        n_heads = 4 if g == "C" else 2
                        dv = N // n_heads
                        for h in range(n_heads):
                            for k in range(t + 1):
                                ins = nc.tensor.matmul(dst[:, h * dv:(h + 1) * dv],
                                                       probs_t[:, h * (t + 1) + k, :],
                                                       values[:, k, h * dv:(h + 1) * dv],
                                                       start=(k == 0), stop=(k == t))
                    ins.then_inc(done, 1)

            def norm_group(nn, g):
                if nn == 0 and g == 0:
                    dst = main[1][:].rearrange("p t n -> p (t n)")
                else:
                    dst = take_aux(("norm", nn, g), (norm_h, 4 * nn + g + 1))
                if g == 0:
                    pe.wait_ge(norm_r, nn + 1)
                for t in range(T):
                    for j in range(4):
                        at, kt = j * S + t * P, 4 * g + j
                        ins = nc.tensor.matmul(dst[:, at:at + P], x_sb[:, t, kt * P:(kt + 1) * P],
                                               r_diag[:, t, :], start=True, stop=True)
                ins.then_inc(norm_t, 1)

            def ff_round(l, q, base, k_end):
                r0 = l * ROUNDS * UP + UP * q
                for k in range(2, k_end):
                    n = base + k
                    up = k % ROUND_UNITS < UP * UNITS
                    j = k // UNITS
                    pe.wait_ge(lo_ready, n + 1)
                    if k in (2, 4, 6):
                        pe.wait_ge(norm_split, 4 * (2 * l + 1) + k // 2 + 1)
                    if k == UNITS:
                        for wait in held:
                            pe.wait_ge(*wait)
                    if k % UNITS == 0:
                        c2 = j - 2
                        if j % 8 in (0, 1, 6, 7):
                            pe.wait_ge(main_free_dve, l * LAYER_DVE_CHUNKS + N_OUT_CHUNKS + UP * q
                                       + (j - 2 - UP if j >= 6 else j - 2) + 1)
                        else:
                            pe.wait_ge(main_free_act, l * LAYER_ACT_CHUNKS + N_IN_CHUNKS + UP * q + c2 + 1)
                    if not up and k % UNITS in (0, 2, 4, 6) and j == UP:
                        pe.wait_ge(hidden_lo, r0 + (k % UNITS) // 2 + 1)
                    left = (act_hi, act_lo) if up else (mid_hi, mid_lo)
                    products(k % SLOTS, left[0], left[1], UNIT_KT * (k % UNITS), k % UNITS == 0,
                             k % UNITS == UNITS - 1, (l * LAYER_CHUNKS + N_IN_CHUNKS + N_OUT_CHUNKS + j) % 2)
                    if k % UNITS == 2 and 1 <= j <= UP:
                        i = j - 1
                        if l == 0 and isinstance(q, int) and q == 0:
                            free = {0: None, 1: None, 2: (mod_ready, round_half(q) + 1), 3: (hidden_lo, r0 + 2)}[i]
                        elif l == 0:
                            free = (mod_ready, round_half(q) - 1 + i) if i < 2 else (hidden_lo, r0 + i - 1)
                        else:
                            free = (hidden_lo, r0 + i - 1)
                        if free is not None:
                            pe.wait_ge(*free)
                        pe.wait_ge(hidden_ready, r0 + i + 1)
                        transposes(aux[(aux0 + i) % 2],
                                   lambda t: stage[:, 0, t * N:(t + 1) * N]).then_inc(hidden_t, 1)
                    if l == 0 and isinstance(q, int) and q == 0:
                        first_round_step(k, r0)
                    elif l == 0 and k in (34, 62):
                        h = 0 if k == 34 else 1
                        pe.wait_ge(hidden_lo, r0 + 3 + h)
                        reduce_into(aux[(aux0 + h) % 2], round_half(q) + h, q, h, 1)

            def first_round_step(k, r0):
                half, a, b = round_half(0), aux[aux0], aux[1 - aux0]
                if k == 20:
                    pe.wait_ge(hidden_lo, r0 + 1)
                    reduce_into(a, half, G2, 0, 0)
                if k == 34:
                    pe.wait_ge(hidden_lo, r0 + 3)
                    reduce_into(a, half + 1, G2, 1, 0)
                if k == 39:
                    pe.wait_ge(mod_ready, half + 2)
                    gate_rows(G2, 0, a).then_inc(gate_sum, 1)
                    pe.wait_ge(hidden_lo, r0 + 4)
                    gate_rows(G2, 1, b).then_inc(gate_sum, 1)
                if k == 50:
                    pe.wait_ge(gate2_ready, 1)
                    reduce_into(a, half + 2, SH1, 0, 1)
                if k == 62:
                    pe.wait_ge(gate2_ready, 2)
                    reduce_into(b, half + 3, SH1, 1, 1)

            def g1_halves(l):
                return HALVES_BEFORE[0] + 2 if l == 0 else round_half(G1) + 2

            pe.wait_ge(ident_ready, 2)
            pe.wait_ge(c_loaded, 16)
            dst = take_aux("c", (c_ready, 1))
            nc.tensor.transpose(dst[:, 0:KT], c_rows[:], ident[0:KT, 0:KT]).then_inc(c_t, 1)
            pe.wait_ge(const_loaded, 32)
            pe.wait_ge(zeroed, 1)
            norm_group(0, 0)
            for half in range(HALVES_BEFORE[0]):
                mod_reduce(half, half // 2, half % 2, 0)
            for l in range(DEPTH):
                if l:
                    norm_group(2 * l, 0)
                norm_group(2 * l, 1)
                plan = mod_halves(l)
                steps = list(PE_SIDE)
                for k in range(STRAIGHT_UNITS):
                    n = l * LAYER_UNITS + k
                    pe.wait_ge(lo_ready, n + 1)
                    if k < IN_UNITS:
                        j, u = divmod(k, UNITS)
                        if u % 2 == 0 and j == 0:
                            pe.wait_ge(norm_split, 4 * 2 * l + u // 2 + 1)
                        left, kt0, first, last = (act_hi, act_lo), UNIT_KT * u, u == 0, u == UNITS - 1
                        width = IN_CHUNKS[IN_NAMES[j]][1]
                        if first:
                            if j >= 2:
                                pe.wait_ge(main_free_act, l * LAYER_ACT_CHUNKS + j - 1)
                            elif l:
                                pe.wait_ge(main_free_dve, l * LAYER_DVE_CHUNKS - 1 + j)
                    else:
                        (j, kt0, first, last), width = OUT_UNITS[k - IN_UNITS], N
                        left = (mid_hi, mid_lo)
                        if first:
                            if j >= 2:
                                pe.wait_ge(main_free_dve, l * LAYER_DVE_CHUNKS + j - 1)
                            else:
                                pe.wait_ge(main_free_act, l * LAYER_ACT_CHUNKS + N_IN_CHUNKS - 1 + j)
                        group = {KT_C: "C", KT_A0: "A0", KT_B: "B", KT_A1: "A1"}.get(kt0)
                        if group and j == 0:
                            after_dve(pe, l, "lo_" + group)
                        j += N_IN_CHUNKS
                    products(k % SLOTS, left[0], left[1], kt0, first, last,
                             (l * LAYER_CHUNKS + j) % 2, width)
                    if k in (1, 3):
                        norm_group(2 * l, 2 + k // 2)
                    while steps and steps[0][1] <= k:
                        side(l, steps.pop(0)[0])
                    if k - 1 in plan and plan[k - 1][3] == HALF_TILES - 1:
                        half, p, h, _ = plan[k - 1]
                        mod_reduce(half, p, h, l)
                assert not steps
                norm_group(2 * l + 1, 0)
                norm_group(2 * l + 1, 1)
                base = l * LAYER_UNITS + STRAIGHT_UNITS
                for k in (0, 1):
                    pe.wait_ge(lo_ready, base + k + 1)
                    if k == 0:
                        pe.wait_ge(norm_split, 4 * (2 * l + 1) + 1)
                        pe.wait_ge(main_free_dve, l * LAYER_DVE_CHUNKS + N_OUT_CHUNKS - 1)
                    products(k, act_hi, act_lo, UNIT_KT * k, k == 0, False,
                             (l * LAYER_CHUNKS + N_IN_CHUNKS + N_OUT_CHUNKS) % 2)
                    norm_group(2 * l + 1, 2 + k)
                if l:
                    for i in (0, 1):
                        dst = take_aux(("gb2", l, i), (gate2_ready, 2 * l + i + 1))
                        if i == 0:
                            pe.wait_ge(mod_ready, HALVES_BEFORE[l] + len(mod_plan(l)))
                        gate_rows(G2, i, dst).then_inc(gate_sum, 1)
                aux0 = taken[0] % 2
                aux_of["rounds", l] = aux0
                if l == 0:
                    ff_round(l, 0, base, ROUND_UNITS + 2)
                with pe.Fori(0 if l else 1, ROUNDS - 1) as q:
                    ff_round(l, q, base + ROUND_UNITS * q, ROUND_UNITS + 2)
                q = ROUNDS - 1
                ff_round(l, q, base + ROUND_UNITS * q, ROUND_UNITS)
                held[aux0] = (mod_ready, round_half(q) + 1) if l == 0 else (hidden_lo, (l + 1) * ROUNDS * UP - 1)
                held[1 - aux0] = (mod_ready, round_half(q) + 2) if l == 0 else (hidden_lo, (l + 1) * ROUNDS * UP)

        @block.scalar
        def _(act):
            links = [0]

            def link(ins):
                links[0] += 1
                ins.then_inc(act_link, 1)
                act.wait_ge(act_link, links[0])

            def round_hi(n, n_over_slots, raw, slot, width=N):
                act.wait_ge(raw_loaded[raw], 16 * (FIRST_LOADS + n_over_slots + 1))
                if not isinstance(n, int) or n >= SLOTS:
                    act.wait_ge(unit_used, n - SLOTS + 1)
                nc.scalar.activation(w_hi[:, slot, :, 0:width], raw_w[:, raw, :, 0:width],
                                     ACT.Copy).then_inc(hi_ready, 1)

            def hi(n):
                k = n % LAYER_UNITS
                width = IN_CHUNKS[IN_NAMES[k // UNITS]][1] if k < IN_UNITS else N
                round_hi(n, n // RAW_SLOTS, n % RAW_SLOTS, n % SLOTS, width)

            def side(l, name):
                done = act_step[l]
                kind, _, what = name.partition("_")
                if step_value(ACT_SIDE, name) > 1:
                    act.wait_ge(done, step_value(ACT_SIDE, name) - 1)
                if kind == "ev":
                    c = IN_NAMES.index(what)
                    bank, width = main[(l * LAYER_CHUNKS + c) % 2], IN_CHUNKS[what][1]
                    act.wait_ge(unit_used, l * LAYER_UNITS + UNITS * (c + 1))
                    if what in ("cv", "av0", "av1"):
                        if what != "cv":
                            after_pe(act, l, {"av0": "oC1", "av1": "oA01"}[what])
                        nc.scalar.activation(values[:], bank[:], ACT.Copy).then_inc(main_free_act, 1)
                        act.wait_ge(main_free_act, l * LAYER_ACT_CHUNKS + c + 1)
                        act.sem_inc(done, 1)
                        return
                    raw = stage[:, 0, :].rearrange("p (t n) -> p t n", t=T)
                    if what == "ik":
                        act.wait_ge(norm_t, 4 * (2 * l + 1))
                    else:
                        after_dve(act, l, prev_reader(what))
                        if what in ROPED or what == "bv":
                            after_pe(act, l, "T_" + prev_transposed(what))
                    nc.scalar.activation(raw[:, :, 0:width], bank[:, :, 0:width],
                                         ACT.Copy).then_inc(main_free_act, 1)
                    act.wait_ge(main_free_act, l * LAYER_ACT_CHUNKS + c + 1)
                    if what in ("ik", "iq"):
                        act.sem_inc(done, 1)
                    elif what in ROPED:
                        for i in range(T * N // DH):
                            cols = slice(i * DH, (i + 1) * DH)
                            ins = nc.scalar.activation(stage[:, 1, cols], stage[:, 0, cols], ACT.Square,
                                                       accum_out=sums[:, i:i + 1])
                        ins.then_inc(done, 1)
                    else:
                        nc.scalar.activation(stage[:, 1, :], stage[:, 0, :], ACT.Square).then_inc(done, 1)
                elif kind == "sc":
                    after_dve(act, l, "rope_" + what)
                    for i in range(T * N // DH):
                        cols = slice(i * DH, (i + 1) * DH)
                        ins = nc.scalar.activation(stage[:, 1, cols], stage[:, 1, cols], ACT.Copy,
                                                   scale=rs[:, i:i + 1])
                    ins.then_inc(done, 1)
                elif kind == "tv":
                    after_pe(act, l, "T_" + what)
                    src = aux[aux_of[l, "T_" + what]][:]
                    if what == "ik":
                        dst, src = idx_keys[:], src[:, 0:2 * S]
                    elif what in ("ck", "ak0", "ak1"):
                        if what != "ck":
                            after_pe(act, l, {"ak0": "sC1", "ak1": "sA01"}[what])
                        dst = keys[:]
                    else:
                        if what != "iq":
                            after_pe(act, l, {"cq": "idx2", "aq0": "sC1", "aq1": "sA01"}[what])
                        dst = queries[:]
                    nc.scalar.activation(dst.rearrange("p a b -> p (a b)"), src, ACT.Copy).then_inc(done, 1)
                elif kind == "tanh":
                    after_dve(act, l, "poly_" + what)
                    nc.scalar.activation(stage[:, 2, :], stage[:, 1, :], ACT.Tanh,
                                         scale=GELU_B).then_inc(done, 1)
                elif kind == "sq":
                    after_dve(act, l, "gelu_bv")
                    nc.scalar.activation(stage[:, 1, :], stage[:, 2, :], ACT.Square).then_inc(done, 1)
                elif kind == "hi":
                    g = what
                    after_pe(act, l, "T_x" + g)
                    kt = {"C": KT_C, "A0": KT_A0, "B": KT_B, "A1": KT_A1}[g]
                    nc.scalar.activation(mid_hi[:, kt:kt + 4, :].rearrange("p a b -> p (a b)"),
                                         aux[aux_of[l, "T_x" + g]][:], ACT.Copy).then_inc(done, 1)
                else:
                    kind, g, t = name[0], name[1:-1], int(name[-1])
                    nk = P * (t + 1)
                    if kind == "e":
                        after_dve(act, l, f"m{g}{t}")
                        for m in range(4):
                            ins = nc.scalar.activation(scores[:, m, 0:nk], scores[:, m, 0:nk], ACT.Exp,
                                                       bias=row_max[:, m:m + 1],
                                                       accum_out=row_sum[:, t, m:m + 1])
                        ins.then_inc(done, 1)
                    elif kind == "t":
                        after_pe(act, l, f"p{g}{t}")
                        if t == 1:
                            after_pe(act, l, f"o{g}0")
                        elif g != "C":
                            after_pe(act, l, {"A0": "oC1", "A1": "oA01"}[g])
                        n = (4 if g == "C" else 2) * (t + 1)
                        nc.scalar.activation(probs_t[:, 0:n, :].rearrange("p a b -> p (a b)"),
                                             aux[aux_of[l, f"p{g}{t}"]][:, 0:n * P],
                                             ACT.Copy).then_inc(done, 1)
                    else:
                        after_pe(act, l, f"o{g}{t}")
                        src = aux[aux_of[l, f"o{g}{t}"]]
                        if t == 0 and g != "C":
                            after_pe(act, l, {"A0": "T_xC", "A1": "T_xA0"}[g])
                        if g == "C":
                            after_dve(act, l, f"i{g}{t}")
                            for h in range(4):
                                ins = nc.scalar.activation(
                                    stage[:, 3, t * N + h * DH:t * N + (h + 1) * DH],
                                    src[:, h * DH:(h + 1) * DH], ACT.Copy, scale=row_inv[:, t, h:h + 1])
                        else:
                            if not (g == "A0" and t == 0):
                                after_dve(act, l, "nA00" if g == "A0" else ("nA01" if t == 0 else "nA10"))
                            nc.scalar.activation(stage[:, 3, t * N:(t + 1) * N], src[:, 0:N], ACT.Copy)
                            for h in range(2):
                                ins = nc.scalar.activation(square[:, h * 2 * DH:(h + 1) * 2 * DH],
                                                           src[:, h * 2 * DH:(h + 1) * 2 * DH], ACT.Square,
                                                           accum_out=head_ss[:, h:h + 1])
                        ins.then_inc(done, 1)

            def mod_columns(half, param, h, src):
                act.wait_ge(mod_reduced, half + 1)
                at = param * KT + h * (MODW // P)
                cols = mod_col[:].rearrange("p a b -> p (a b)")
                nc.scalar.activation(cols[:, bass.ds(at, MODW // P)], src[:, 0:MODW // P],
                                     ACT.Copy).then_inc(mod_ready, 1)

            def squares(nn, j):
                if nn == 0:
                    act.wait_ge(x_loaded, 16 * T)
                else:
                    last_round = (ROUNDS - 1) * UP if nn % 2 == 0 else -N_OUT_CHUNKS
                    act.wait_ge(x_ready, ((nn - 1) // 2) * LAYER_DVE_CHUNKS + N_OUT_CHUNKS + last_round + j + 1)
                if nn or j:
                    act.wait_ge(norm_ss, nn * (D // N) + j)
                for t in range(T):
                    junk = probs_t[:, 4 * t:4 * t + 4, :].rearrange("p a b -> p (a b)")
                    ins = nc.scalar.activation(junk, x_sb[:, t, j * N:(j + 1) * N], ACT.Square,
                                               accum_out=row_parts[:, j, t:t + 1])
                ins.then_inc(norm_ss, 1)

            def norm(nn, unit):
                second = nn % 2
                shift = SH2 if second else SH1

                def modulate(g):
                    act.wait_ge(norm_t, 4 * nn + g + 1)
                    if g == 0:
                        act.wait_ge(norm_scale, nn + 1)
                    if g >= 2:
                        act.wait_ge(norm_split, 4 * nn + g - 1)
                    if nn == 0 and g == 0:
                        src = main[1][:].rearrange("p t n -> p (t n)")
                    else:
                        src = aux[aux_of["norm", nn, g]]
                    for j in range(4):
                        kt = 4 * g + j
                        ins = nc.scalar.activation(stage[:, 2 + g % 2, j * S:(j + 1) * S],
                                                   src[:, j * S:(j + 1) * S], ACT.Identity,
                                                   bias=mod_col[:, shift, kt:kt + 1],
                                                   scale=scale_col[:, kt:kt + 1])
                    ins.then_inc(norm_h, 1)

                for g in range(4):
                    modulate(g)
                    for k in units_beside(nn, g):
                        hi(unit + k)

            def ff_round(l, q, base, last=False):
                r0 = l * ROUNDS * UP + UP * q
                for k in range(SLOTS, ROUND_UNITS + (2 + AHEAD if last else SLOTS)):
                    if not last or k < ROUND_UNITS:
                        round_hi(base + k, (l * LAYER_UNITS + STRAIGHT_UNITS) // RAW_SLOTS
                                 + (ROUND_UNITS // RAW_SLOTS) * q + k // RAW_SLOTS, k % RAW_SLOTS, k % SLOTS)
                    elif l < DEPTH - 1:
                        hi(base + k)
                    j, u = divmod(k - AHEAD, UNITS)
                    if u == 1 and 1 <= j <= UP:
                        i = j - 1
                        bank = main[(l * LAYER_CHUNKS + N_IN_CHUNKS + N_OUT_CHUNKS + i) % 2]
                        act.wait_ge(unit_used, base + UNITS * j)
                        nc.scalar.activation(stage[:, 0, :], bank[:].rearrange("p t n -> p (t n)"),
                                             ACT.Relu).then_inc(main_free_act, 1)
                        act.wait_ge(main_free_act,
                                    l * LAYER_ACT_CHUNKS + N_IN_CHUNKS + UP * q + i + 1)
                        nc.scalar.activation(stage[:, 0, :], stage[:, 0, :],
                                             ACT.Square).then_inc(hidden_ready, 1)
                    if u == 3 and 1 <= j <= UP:
                        i = j - 1
                        act.wait_ge(hidden_t, r0 + i + 1)
                        nc.scalar.activation(mid_hi[:, 4 * i:4 * i + 4, :].rearrange("p a b -> p (a b)"),
                                             aux[(aux_of["rounds", l] + i) % 2][:],
                                             ACT.Copy).then_inc(hidden_hi, 1)
                    if l == 0 and isinstance(q, int) and q == 0:
                        made = {21: (0, G2, 0), 35: (1, G2, 0), 51: (2, SH1, 0), 63: (3, SH1, 1)}
                        if k - AHEAD in made:
                            h, param, buf = made[k - AHEAD]
                            mod_columns(round_half(0) + h, param, h % 2, aux[(aux_of["rounds", 0] + buf) % 2])
                    elif l == 0 and k - AHEAD in (35, 63):
                        h = 0 if k - AHEAD == 35 else 1
                        mod_columns(round_half(q) + h, q, h, aux[(aux_of["rounds", l] + h) % 2])
                    if last and l < DEPTH - 1 and j > UP and u == (3 if j < 2 * UP else 1):
                        squares(2 * l + 2, j - 1 - UP)

            def prev_reader(what):
                order = ["ik", "iq", "ck", "cq", "ak0", "aq0", "ak1", "aq1", "bv", "bu"]
                before = order[order.index(what) - 1]
                return {"bv": "norm_bv"}.get(before, "rope_" + before)

            def prev_transposed(what):
                order = ["ik", "iq", "ck", "cq", "ak0", "aq0", "ak1", "aq1", "bv"]
                return order[order.index(what) - 1]

            act.wait_ge(c_t, 1)
            nc.scalar.activation(c_exp[:], aux[aux_of["c"]][:, 0:KT], ACT.Exp,
                                 scale=-1.0).then_inc(c_exp_ready, 1)
            for j in range(D // N):
                squares(0, j)
            act.wait_ge(lam_dots, 1)
            nc.scalar.activation(lam[:], lam[:], ACT.Exp).then_inc(lam_exp, 1)
            for l in range(DEPTH):
                first = l * LAYER_UNITS
                if l == 0:
                    for half in range(FIRST_HALVES):
                        if half == FIRST_HALVES - 1:
                            for k in units_beside(0, -1):
                                hi(k)
                        mod_columns(half, half // 2, half % 2, aux[aux_of["mod", half]])
                norm(2 * l, first)
                steps, plan = list(ACT_SIDE), mod_halves(l)
                for k in range(SLOTS, STRAIGHT_UNITS + 2 + AHEAD):
                    hi(first + k)
                    if k - 2 - AHEAD in plan and plan[k - 2 - AHEAD][3] == HALF_TILES - 1:
                        half, p, h, _ = plan[k - 2 - AHEAD]
                        mod_columns(half, p, h, aux[aux_of["mod", half]])
                    while steps and steps[0][1] <= k:
                        side(l, steps.pop(0)[0])
                    if k in finished:
                        squares(2 * l + 1, finished[k])
                assert not steps
                norm(2 * l + 1, first + STRAIGHT_UNITS)
                base = first + STRAIGHT_UNITS
                if l == 0:
                    ff_round(l, 0, base)
                with act.Fori(0 if l else 1, ROUNDS - 1) as q:
                    ff_round(l, q, base + ROUND_UNITS * q)
                q = ROUNDS - 1
                ff_round(l, q, base + ROUND_UNITS * q, last=True)

        @block.vector
        def _(dve):
            links = [0]
            V = nc.vector

            def link(ins):
                links[0] += 1
                ins.then_inc(dve_link, 1)
                dve.wait_ge(dve_link, links[0])

            def lo(n, raw, slot, width=N):
                dve.wait_ge(hi_ready, n + 1)
                V.tensor_tensor(w_lo[:, slot, :, 0:width], raw_w[:, raw, :, 0:width],
                                w_hi[:, slot, :, 0:width].bitcast(F32), ALU.subtract).then_inc(lo_ready, 1)

            def straight_lo(n):
                k = n % LAYER_UNITS
                width = IN_CHUNKS[IN_NAMES[k // UNITS]][1] if k < IN_UNITS else N
                lo(n, n % RAW_SLOTS, n % SLOTS, width)

            def mod_tile(half, h, kt):
                m = HALF_TILES * half + kt
                if isinstance(half, int) and half < FIRST_HALVES:
                    slot = m % RAW_SLOTS
                    dve.wait_ge(raw_loaded[slot], 16 * (m // RAW_SLOTS + 1))
                    tile = raw_w[:, slot, :, :].rearrange("p s n -> p (s n)")
                else:
                    slot, before = mod_slot(half, kt)
                    dve.wait_ge(mod_loaded[slot], 16 * (before + 1))
                    tile = raw_mod[:, slot, :]
                acc = mod_acc[:, h, :]
                if kt == 0:
                    if not isinstance(half, int) or half >= 2:
                        dve.wait_ge(mod_reduced, half - 1)
                    V.tensor_scalar(acc, tile, c_act[:, 0:1], None, ALU.mult).then_inc(mod_used, 1)
                else:
                    dve.wait_ge(mod_used, m)
                    V.scalar_tensor_tensor(out=acc, in0=tile, scalar=c_act[:, kt:kt + 1], in1=acc,
                                           op0=ALU.mult, op1=ALU.add).then_inc(mod_used, 1)

            def rsqrt(out, ss, inv_n, n):
                v, g, w = newton[:, 0, 0:n], newton[:, 1, 0:n], newton[:, 2, 0:n]
                bits = newton_i[:, 0:n]
                link(V.tensor_scalar(v, ss, inv_n, EPS, ALU.mult, ALU.add))
                link(V.tensor_scalar(bits, v.bitcast(I32), 1, None, ALU.logical_shift_right))
                link(V.tensor_scalar(bits, bits, -1.0, float(0x5F3759DF), ALU.mult, ALU.add))
                for i in range(3):
                    link(V.tensor_tensor(w, g, g, ALU.mult))
                    link(V.scalar_tensor_tensor(out=w, in0=w, scalar=-0.5, in1=v, op0=ALU.mult, op1=ALU.mult))
                    last = V.scalar_tensor_tensor(out=out if i == 2 else g, in0=w, scalar=1.5, in1=g,
                                                  op0=ALU.add, op1=ALU.mult)
                    if i < 2:
                        link(last)
                return last

            def heads(i, n_heads, dh, c0=0, c1=None):
                v = stage[:, i, :].rearrange("p (t h d) -> p t h d", t=T, h=n_heads)
                return v[:, :, :, c0:dh if c1 is None else c1]

            def over_heads(table, n_heads):
                shape = list(table.shape)
                return table.unsqueeze(2).broadcast_to([P, shape[1], n_heads, shape[2]])

            def side(l, name):
                done = dve_step[l]
                kind, _, what = name.partition("_")
                if step_value(DVE_SIDE, name) > 1:
                    dve.wait_ge(done, step_value(DVE_SIDE, name) - 1)
                if name == "ws_mask":
                    dve.wait_ge(gains_loaded[l], 16 * 8)
                    V.memset(ws_raw[0:CHUNK, :, CHUNK:P], 0.0)
                    V.tensor_scalar(sub_gain[:], sub_gain[:], 1.0 - (0.8 - 0.6 * math.exp(-0.3 * l)), None,
                                    ALU.mult).then_inc(done, 1)
                elif name == "ws":
                    after_pe(dve, l, "T_ws")
                    src = aux[aux_of[l, "T_ws"]]
                    V.tensor_copy(ws_t[:].rearrange("p a b -> p (a b)"), src[:, 0:N])
                    V.tensor_copy(bias_t[:], src[:, N:N + 4]).then_inc(done, 1)
                elif name == "rope_ik":
                    after_act(dve, l, "ev_ik")
                    raw = stage[:, 0, :].rearrange("p (t n) -> p t n", t=T)
                    work = stage[:, 2, :].rearrange("p (t n) -> p t n", t=T)
                    half = IDX_DH // 2
                    link(V.memset(stage[:, 1, 0:2 * S], 0.0))
                    V.tensor_scalar(idx_w[:], raw[:, :, IDX_DH:IDX_DH + IDX_HEADS], IDX_SCALE, None, ALU.mult)
                    V.tensor_tensor(work[:, :, 0:IDX_DH], raw[:, :, 0:IDX_DH], cos64, ALU.mult)
                    V.tensor_tensor(work[:, :, IDX_DH:IDX_DH + half], raw[:, :, half:IDX_DH],
                                    sin64[:, :, 0:half], ALU.mult)
                    link(V.tensor_tensor(work[:, :, IDX_DH + half:2 * IDX_DH], raw[:, :, 0:half],
                                         sin64[:, :, half:IDX_DH], ALU.mult))
                    pair = stage[:, 1, 0:2 * S].rearrange("p (t n) -> p t n", t=T)
                    for at in (0, P + IDX_DH):
                        ins = V.tensor_tensor(pair[:, :, at:at + IDX_DH], work[:, :, 0:IDX_DH],
                                              work[:, :, IDX_DH:2 * IDX_DH], ALU.add)
                    ins.then_inc(done, 1)
                elif name == "rope_iq":
                    after_act(dve, l, "ev_iq")
                    after_pe(dve, l, "T_ik")
                    half, nh = IDX_DH // 2, IDX_HEADS
                    V.tensor_tensor(heads(1, nh, IDX_DH), heads(0, nh, IDX_DH), over_heads(cos64, nh), ALU.mult)
                    V.tensor_tensor(heads(2, nh, IDX_DH, 0, half), heads(0, nh, IDX_DH, half),
                                    over_heads(sin64[:, :, 0:half], nh), ALU.mult)
                    link(V.tensor_tensor(heads(2, nh, IDX_DH, half), heads(0, nh, IDX_DH, 0, half),
                                         over_heads(sin64[:, :, half:], nh), ALU.mult))
                    V.tensor_tensor(stage[:, 1, :], stage[:, 1, :], stage[:, 2, :], ALU.add).then_inc(done, 1)
                elif kind == "rs" and what != "bv":
                    after_act(dve, l, "ev_" + what)
                    rsqrt(rs[:, 0:8], sums[:, 0:8], 1.0 / DH, 8).then_inc(done, 1)
                elif kind == "mul":
                    gain = qk_gain[:, {"aq": 0, "ak": 1, "cq": 2, "ck": 3}[what[:2]], :]
                    half = DH // 2

                    def over_t(x):
                        return x.unsqueeze(1).broadcast_to([P, T, x.shape[1]])
                    V.tensor_tensor(gained[:, 0, :, :], cos128, over_t(gain), ALU.mult)
                    V.tensor_tensor(gained[:, 1, :, 0:half], sin128[:, :, 0:half], over_t(gain[:, half:]), ALU.mult)
                    link(V.tensor_tensor(gained[:, 1, :, half:], sin128[:, :, half:], over_t(gain[:, 0:half]),
                                         ALU.mult))
                    V.tensor_tensor(heads(1, 4, DH), heads(0, 4, DH), over_heads(gained[:, 0, :, :], 4),
                                    ALU.mult).then_inc(done, 1)
                elif kind == "rope":
                    half = DH // 2
                    V.tensor_tensor(heads(2, 4, DH, 0, half), heads(0, 4, DH, half),
                                    over_heads(gained[:, 1, :, 0:half], 4), ALU.mult)
                    link(V.tensor_tensor(heads(2, 4, DH, half), heads(0, 4, DH, 0, half),
                                         over_heads(gained[:, 1, :, half:], 4), ALU.mult))
                    V.tensor_tensor(stage[:, 1, :], stage[:, 1, :], stage[:, 2, :], ALU.add).then_inc(done, 1)
                elif kind[:3] == "isc":
                    i = int(name[3])
                    after_pe(dve, l, f"idx{i}")
                    t = 0 if i == 0 else 1
                    nh, nk, h0 = (8, P, 0) if i == 0 else (4, S, 4 * i - 4)
                    work = scores[:].rearrange("p a b -> p (a b)").rearrange("p (h k) -> p h k", h=nh)
                    src = aux[aux_of[l, f"idx{i}"]][:].rearrange("p (h k) -> p h k", h=nh)
                    link(V.scalar_tensor_tensor(out=work, in0=src, scalar=0.0,
                                                in1=idx_w[:, t, h0:h0 + nh].unsqueeze(2).broadcast_to([P, nh, nk]),
                                                op0=ALU.max, op1=ALU.mult))
                    dst = mask[:, t, 0:nk] if i < 2 else gained[:].rearrange("p a b c -> p (a b c)")[:, 0:nk]
                    red = V.tensor_reduce(dst, work.rearrange("p h k -> p k h"), AX.X, ALU.add)
                    if i == 2:
                        link(red)
                        red = V.tensor_tensor(mask[:, 1, :], mask[:, 1, :], dst, ALU.add)
                    red.then_inc(done, 1)
                elif kind[:4] == "topk":
                    t = int(name[4])
                    nk = P * (t + 1)
                    dve.wait_ge(done, step_value(DVE_SIDE, f"isc{2 * t}"))
                    link(V.memset(mask[0:CHUNK, t, nk - CHUNK:nk], NEG))
                    src = mask[:, t, 0:nk]
                    for r in range(TOPK // 8):
                        dst = scores[:, 2 * t + r % 2, 0:nk]
                        link(V.max(top8[:], src))
                        rep = V.match_replace(dst, top8[:], src, TAKEN)
                        if r < TOPK // 8 - 1:
                            link(rep)
                        src = dst
                    rep.then_inc(done, 1)
                elif name == "mask":
                    dve.wait_ge(done, step_value(DVE_SIDE, "topk1"))
                    for t in range(T):
                        nk = P * (t + 1)
                        left = scores[:, 2 * t + 1, 0:nk]
                        link(V.tensor_scalar(left, left, TAKEN, None, ALU.is_equal))
                        link(V.scalar_tensor_tensor(out=left, in0=mask[:, t, 0:nk], scalar=0.5 * NEG, in1=left,
                                                    op0=ALU.is_gt, op1=ALU.mult))
                        ins = V.tensor_scalar(mask[:, t, 0:nk], left, -1.0, -NEG, ALU.add, ALU.mult)
                        if t == 0:
                            link(ins)
                    ins.then_inc(done, 1)
                elif name == "maskA":
                    link(V.memset(mask[:], 0.0))
                    V.memset(mask[0:CHUNK, 0, CHUNK:P], NEG)
                    V.memset(mask[0:CHUNK, 1, S - CHUNK:S], NEG).then_inc(done, 1)
                elif kind == "g":
                    i = int(what)
                    after_pe(dve, l, f"gb_{i}")
                    V.tensor_copy(gate[:, i * 1024:(i + 1) * 1024],
                                  aux[aux_of[l, f"gb_{i}"]][:]).then_inc(done, 1)
                elif kind == "poly":
                    after_act(dve, l, "ev_" + what)
                    link(V.tensor_scalar(stage[:, 1, :], stage[:, 1, :], GELU_A, 1.0, ALU.mult, ALU.add))
                    V.tensor_tensor(stage[:, 1, :], stage[:, 1, :], stage[:, 0, :], ALU.mult).then_inc(done, 1)
                elif kind == "gelu":
                    after_act(dve, l, "tanh_" + what)
                    link(V.scalar_tensor_tensor(out=stage[:, 2, :], in0=stage[:, 2, :], scalar=1.0,
                                                in1=stage[:, 0, :], op0=ALU.add, op1=ALU.mult))
                    V.tensor_scalar(stage[:, 2, :], stage[:, 2, :], 0.5, None, ALU.mult).then_inc(done, 1)
                elif name == "rs_bv":
                    after_act(dve, l, "sq_bv")
                    link(V.tensor_reduce(sums[:, 0:8], stage[:, 1, :].rearrange("p (a b) -> p a b", b=P),
                                         AX.X, ALU.add))
                    link(rsqrt(rs[:, 0:8], sums[:, 0:8], 1.0 / P, 8))
                    flat = stage[:, 2, :].rearrange("p (a b) -> p a b", b=P)
                    V.tensor_tensor(flat, flat, rs[:, 0:8].unsqueeze(2).broadcast_to([P, 8, P]),
                                    ALU.mult).then_inc(done, 1)
                elif name == "norm_bv":
                    dve.wait_ge(done, step_value(DVE_SIDE, "rs_bv"))
                    after_pe(dve, l, "sA11")
                    V.tensor_tensor(queries[:].rearrange("p a b -> p (a b)").rearrange("p (t n) -> p t n", t=T),
                                    stage[:, 2, :].rearrange("p (t n) -> p t n", t=T),
                                    v_gain[:].unsqueeze(1).broadcast_to([P, T, N]), ALU.mult).then_inc(done, 1)
                elif name == "gate_B":
                    after_pe(dve, l, "z_B")
                    dve.wait_ge(done, step_value(DVE_SIDE, "gelu_bu"))
                    z = aux[aux_of[l, "z_B"]][:].rearrange("p (t g c) -> p t g c", t=T, g=4)
                    for g in range(4):
                        ins = V.scalar_tensor_tensor(out=heads(1, 4, P)[:, :, g, :], in0=z[:, :, g, :],
                                                     scalar=bias_t[:, g:g + 1], in1=heads(2, 4, P)[:, :, g, :],
                                                     op0=ALU.add, op1=ALU.mult)
                    ins.then_inc(done, 1)
                elif kind == "lo":
                    g = what
                    after_act(dve, l, "hi_" + g)
                    kt = {"C": KT_C, "A0": KT_A0, "B": KT_B, "A1": KT_A1}[g]
                    V.tensor_tensor(mid_lo[:, kt:kt + 4, :].rearrange("p a b -> p (a b)"),
                                    aux[aux_of[l, "T_x" + g]][:],
                                    mid_hi[:, kt:kt + 4, :].bitcast(F32).rearrange("p a b -> p (a b)"),
                                    ALU.subtract).then_inc(done, 1)
                else:
                    kind, g, t = name[0], name[1:-1], int(name[-1])
                    nk = P * (t + 1)
                    if kind == "m":
                        after_pe(dve, l, f"s{g}{t}")
                        if t == 1:
                            after_pe(dve, l, f"p{g}0")
                        elif g != "C":
                            after_pe(dve, l, {"A0": "pC1", "A1": "pA01"}[g])
                        src = aux[aux_of[l, f"s{g}{t}"]][:, 0:4 * nk].rearrange("p (m k) -> p m k", m=4)
                        link(V.scalar_tensor_tensor(out=scores[:, :, 0:nk], in0=src, scalar=QK_SCALE,
                                                    in1=mask[:, t, 0:nk].unsqueeze(1).broadcast_to([P, 4, nk]),
                                                    op0=ALU.mult, op1=ALU.add))
                        V.tensor_reduce(row_max[:], scores[:, :, 0:nk], AX.X, ALU.max,
                                        negate=True).then_inc(done, 1)
                    elif kind == "i":
                        after_act(dve, l, f"e{g}{t}")
                        V.reciprocal(row_inv[:, t, :], row_sum[:, t, :]).then_inc(done, 1)
                    elif kind == "c":
                        after_act(dve, l, f"e{g}{t}")
                        link(V.reciprocal(row_inv[:, t, :], row_sum[:, t, :]))
                        odd = row_inv[:, t, :].rearrange("p (h m) -> p h m", m=2)[:, :, 1]
                        link(V.tensor_scalar(odd, odd, neg_lam[:, l:l + 1], None, ALU.mult))
                        for m in (0, 2):
                            link(V.tensor_scalar(scores[:, m, 0:nk], scores[:, m, 0:nk],
                                                 row_inv[:, t, m:m + 1], None, ALU.mult))
                            ins = V.scalar_tensor_tensor(out=scores[:, m, 0:nk], in0=scores[:, m + 1, 0:nk],
                                                         scalar=row_inv[:, t, m + 1:m + 2],
                                                         in1=scores[:, m, 0:nk], op0=ALU.mult, op1=ALU.add)
                        ins.then_inc(done, 1)
                    else:
                        after_act(dve, l, f"v{g}{t}")
                        link(rsqrt(rs[:, 8:10], head_ss[:], 1.0 / (2 * DH), 2))
                        for h in range(2):
                            at = t * N + h * 2 * DH
                            ins = V.scalar_tensor_tensor(out=stage[:, 3, at:at + 2 * DH],
                                                         in0=stage[:, 3, at:at + 2 * DH],
                                                         scalar=rs[:, 8 + h:9 + h], in1=sub_gain[:],
                                                         op0=ALU.mult, op1=ALU.mult)
                        ins.then_inc(done, 1)

            def scale(nn):
                V.tensor_scalar(scale_col[:], mod_col[:, SC2 if nn % 2 else SC1, :], 1.0, None,
                                ALU.add).then_inc(norm_scale, 1)

            def norm(nn):
                if nn:
                    scale(nn)
                dve.wait_ge(norm_ss, (nn + 1) * (D // N))
                link(V.tensor_reduce(row_ss[:], row_parts[:].rearrange("p j t -> p t j"), AX.X, ALU.add))
                link(rsqrt(row_r[:], row_ss[:], 1.0 / D, T))
                for t in range(T):
                    ins = V.tensor_scalar(r_diag[:, t, :], ident[:], row_r[:, t:t + 1], None, ALU.mult)
                ins.then_inc(norm_r, 1)

            def split(nn, unit):
                for g in range(4):
                    dve.wait_ge(norm_h, 4 * nn + g + 1)
                    rows = stage[:, 2 + g % 2, :].rearrange("p (a b) -> p a b", a=4)
                    kts = slice(4 * g, 4 * g + 4)
                    link(V.tensor_copy(act_hi[:, kts, :], rows))
                    V.tensor_tensor(act_lo[:, kts, :], rows, act_hi[:, kts, :].bitcast(F32),
                                    ALU.subtract).then_inc(norm_split, 1)
                    for k in units_beside(nn, g):
                        straight_lo(unit + k)

            def gate_chunk(bank, j, used, before):
                dve.wait_ge(unit_used, used)
                if before is not None:
                    dve.wait_ge(x_ready, before)
                V.tensor_tensor(stage[:, 2, :].rearrange("p (t n) -> p t n", t=T), main[bank][:],
                                gate[:, j * N:(j + 1) * N].unsqueeze(1).broadcast_to([P, T, N]),
                                ALU.mult).then_inc(main_free_dve, 1)

            def add_chunk(j, count):
                cols = slice(j * N, (j + 1) * N)
                dve.wait_ge(main_free_dve, count)
                V.tensor_tensor(x_sb[:, :, cols], x_sb[:, :, cols],
                                stage[:, 2, :].rearrange("p (t n) -> p t n", t=T), ALU.add).then_inc(x_ready, 1)

            def ff_round(l, q, base, last=False):
                r0 = l * ROUNDS * UP + UP * q
                for k in range(SLOTS, ROUND_UNITS + (2 + AHEAD if last else SLOTS)):
                    if not last or k < ROUND_UNITS:
                        lo(base + k, k % RAW_SLOTS, k % SLOTS)
                    elif l < DEPTH - 1:
                        straight_lo(base + k)
                    j, u = divmod(k - AHEAD, UNITS)
                    for _, half, _, h, kt in round_tiles(l, q, k):
                        mod_tile(half, h, kt)
                    if u == 4 and 1 <= j <= UP:
                        i = j - 1
                        dve.wait_ge(hidden_hi, r0 + i + 1)
                        V.tensor_tensor(mid_lo[:, 4 * i:4 * i + 4, :].rearrange("p a b -> p (a b)"),
                                        aux[(aux_of["rounds", l] + i) % 2][:],
                                        mid_hi[:, 4 * i:4 * i + 4, :].bitcast(F32).rearrange("p a b -> p (a b)"),
                                        ALU.subtract).then_inc(hidden_lo, 1)
                    if l == 0 and isinstance(q, int) and q == 0:
                        if k - AHEAD in (40, 41):
                            i = k - AHEAD - 40
                            gate2_rows(0, i, aux[(aux_of["rounds", 0] + i) % 2])
                    if u == 1 and j > UP:
                        gate_down(l, q, base, j - 1)
                    if j > UP and u == (2 if j < 2 * UP else 1):
                        add_down(l, q, j - 1)

            def gate2_rows(l, i, src):
                dve.wait_ge(gate_sum, 2 * l + i + 1)
                V.tensor_copy(gate[:, i * 1024:(i + 1) * 1024], src[:]).then_inc(gate2_ready, 1)
                if i == 1:
                    dve.wait_ge(gate2_ready, 2 * l + 2)

            def down_count(l, q, j):
                return l * LAYER_DVE_CHUNKS + N_OUT_CHUNKS + UP * q + j - UP

            def gate_down(l, q, base, j):
                gate_chunk((l * LAYER_CHUNKS + N_IN_CHUNKS + N_OUT_CHUNKS + j) % 2, j - UP,
                           base + UNITS * (j + 1), down_count(l, q, j))

            def add_down(l, q, j):
                add_chunk(j - UP, down_count(l, q, j) + 1)

            dve.wait_ge(lam_loaded, 16)
            prod = stage[:, 2, 0:DEPTH * 2 * DH].rearrange("p (a b) -> p a b", b=DH)
            both = stage[:, 1, 0:DEPTH * 4 * DH].rearrange("p (a m b) -> p a m b", m=2, b=DH)
            link(V.tensor_tensor(prod, both[:, :, 0, :], both[:, :, 1, :], ALU.mult))
            V.tensor_reduce(lam[:], prod, AX.X, ALU.add).then_inc(lam_dots, 1)
            dve.wait_ge(c_exp_ready, 1)
            link(V.tensor_copy(c_raw[:], aux[aux_of["c"]][:, 0:KT]))
            link(V.tensor_scalar(c_exp[:], c_exp[:], 1.0, None, ALU.add))
            link(V.reciprocal(c_exp[:], c_exp[:]))
            V.tensor_tensor(c_act[:], c_raw[:], c_exp[:], ALU.mult).then_inc(c_ready, 1)
            dve.wait_ge(c_ready, 1)
            dve.wait_ge(lam_exp, 1)
            for l in range(DEPTH):
                link(V.tensor_tensor(neg_lam[:, l:l + 1], lam[:, 2 * l + 1:2 * l + 2], lam[:, 2 * l:2 * l + 1],
                                     ALU.subtract))
                link(V.tensor_scalar(neg_lam[:, l:l + 1], neg_lam[:, l:l + 1],
                                     -(0.8 - 0.6 * math.exp(-0.3 * l)), None, ALU.add))
            norm(0)
            for half in range(HALVES_BEFORE[0]):
                for kt in range(HALF_TILES):
                    mod_tile(half, half % 2, kt)
            for l in range(DEPTH):
                first = l * LAYER_UNITS
                if l == 0:
                    for k in units_beside(0, -1):
                        straight_lo(k)
                dve.wait_ge(mod_ready, HALVES_BEFORE[l])
                if l:
                    norm(2 * l)
                else:
                    scale(0)
                split(2 * l, first)
                plan = mod_halves(l)
                steps = list(DVE_SIDE)
                for k in range(SLOTS, STRAIGHT_UNITS + 2 + AHEAD):
                    straight_lo(first + k)
                    if k in plan:
                        half, p, h, kt = plan[k]
                        mod_tile(half, h, kt)
                    if k in finished:
                        j = finished[k]
                        count = l * LAYER_DVE_CHUNKS + j
                        gate_chunk((l * LAYER_CHUNKS + N_IN_CHUNKS + j) % 2, j, first + k - 1 - AHEAD,
                                   count or None)
                        add_chunk(j, count + 1)
                    while steps and steps[0][1] <= k:
                        side(l, steps.pop(0)[0])
                assert not steps
                dve.wait_ge(mod_ready, HALVES_BEFORE[l] + len(mod_plan(l)))
                norm(2 * l + 1)
                split(2 * l + 1, first + STRAIGHT_UNITS)
                if l:
                    for i in (0, 1):
                        gate2_rows(l, i, aux[aux_of["gb2", l, i]])
                base = first + STRAIGHT_UNITS
                if l == 0:
                    ff_round(l, 0, base)
                with dve.Fori(0 if l else 1, ROUNDS - 1) as q:
                    ff_round(l, q, base + ROUND_UNITS * q)
                q = ROUNDS - 1
                ff_round(l, q, base + ROUND_UNITS * q, last=True)

        @block.gpsimd
        def _(pool):
            nc.gpsimd.memset(ident[:], 0.0).then_inc(ident_ready, 1)
            nc.gpsimd.memset(ones[:], 1.0).then_inc(zeroed, 1)
            pool.wait_ge(ident_ready, 1)
            nc.gpsimd.affine_select(out=ident[:], in_=ident[:], compare_op=ALU.not_equal, fill=1.0, base=0,
                                    pattern=[[-1, P]], channel_multiplier=1).then_inc(ident_ready, 1)

        @block.sync
        def _(sp):
            def load_unit(n, slot, src):
                if not isinstance(n, int) or n >= RAW_SLOTS:
                    sp.wait_ge(lo_ready, n - RAW_SLOTS + 1)
                else:
                    sp.wait_ge(mod_used, HALF_TILES * FIRST_HALVES - RAW_SLOTS + n + 1)
                width = src.shape[-1]
                sp.dma_start(raw_w[:, slot, :, 0:width],
                             src.rearrange("(s p) n -> p s n", p=P)).then_inc(raw_loaded[slot], 16)

            def load_mod(l, half, param, h, kt):
                m = HALF_TILES * half + kt
                if isinstance(half, int) and half < FIRST_HALVES:
                    n_slots, slot = RAW_SLOTS, m % RAW_SLOTS
                    tile, loaded = raw_w[:, slot, :, :].rearrange("p s n -> p (s n)"), raw_loaded[slot]
                else:
                    n_slots, (slot, _) = MOD_SLOTS, mod_slot(half, kt)
                    tile, loaded = raw_mod[:, slot, :], mod_loaded[slot]
                if not isinstance(half, int) or m >= n_slots:
                    sp.wait_ge(mod_used, m - n_slots + 1)
                src = w_mod[l, kt * P:(kt + 1) * P, bass.ds(param * D + h * MODW, MODW)]
                sp.dma_start(tile, src).then_inc(loaded, 16)

            sp.dma_start(c_rows[:], c[0, :].rearrange("(a b) -> a b", b=P)).then_inc(c_loaded, 16)
            sp.dma_start(stage[:, 1, 0:DEPTH * 4 * DH],
                         a_lambda.rearrange("l m d -> (l m d)").partition_broadcast(P)).then_inc(lam_loaded, 16)
            sp.dma_start(b_mod_sb[:], b_mod.rearrange("l (r c) -> r l c", c=P)).then_inc(const_loaded, 16)
            sp.dma_start(rope_sb[:], rope.rearrange("(t p) n -> p t n", p=P)).then_inc(const_loaded, 16)
            for t in range(T):
                sp.dma_start(x_sb[:, t, :], x[0, t * P:(t + 1) * P, :]).then_inc(x_loaded, 16)
            for half in range(HALVES_BEFORE[0]):
                for kt in range(HALF_TILES):
                    load_mod(0, half, half // 2, half % 2, kt)
            for l in range(DEPTH):
                if l:
                    after_pe(sp, l - 1, PE_SIDE[-1][0])
                    after_act(sp, l - 1, ACT_SIDE[-1][0])
                    after_dve(sp, l - 1, DVE_SIDE[-1][0])
                loaded = gains_loaded[l]
                for i, gain in enumerate((a_qnorm, a_knorm, c_qnorm, c_knorm)):
                    sp.dma_start(qk_gain[:, i, :], gain[l, :].partition_broadcast(P)).then_inc(loaded, 16)
                sp.dma_start(sub_gain[:], a_subln[l, :].partition_broadcast(P)).then_inc(loaded, 16)
                sp.dma_start(v_gain[:], b_vnorm[l, :].partition_broadcast(P)).then_inc(loaded, 16)
                sp.dma_start(ws_raw[:], b_ws[l].rearrange("g i j -> i g j")).then_inc(loaded, 16)
                sp.dma_start(bias_raw[:], b_bias[l]).then_inc(loaded, 16)
                plan = mod_halves(l)
                for k in range(STRAIGHT_UNITS):
                    n = l * LAYER_UNITS + k
                    if k < IN_UNITS:
                        j, u = divmod(k, UNITS)
                        col, width = IN_CHUNKS[IN_NAMES[j]]
                        src = w_in[l, UNIT_KT * P * u:UNIT_KT * P * (u + 1), col:col + width]
                    else:
                        j, kt0, _, _ = OUT_UNITS[k - IN_UNITS]
                        src = w_out[l, kt0 * P:(kt0 + UNIT_KT) * P, j * N:(j + 1) * N]
                    load_unit(n, n % RAW_SLOTS, src)
                    if k - MOD_BEHIND in plan:
                        load_mod(l, *plan[k - MOD_BEHIND])
                base = l * LAYER_UNITS + STRAIGHT_UNITS

                def ff_round(q):
                    for k in range(ROUND_UNITS):
                        j, u = divmod(k, UNITS)
                        if j < UP:
                            src = w_ff1[l, UNIT_KT * P * u:UNIT_KT * P * (u + 1), bass.ds(q * D + j * N, N)]
                        else:
                            src = w_ff2[l, bass.ds(q * D + UNIT_KT * P * u, UNIT_KT * P),
                                        (j - UP) * N:(j - UP + 1) * N]
                        load_unit(base + ROUND_UNITS * q + k, k % RAW_SLOTS, src)
                        last = k == ROUND_UNITS - 1
                        for at in range(k - MOD_BEHIND, k + 1 if last else k - MOD_BEHIND + 1):
                            for tile in round_tiles(l, q, at):
                                load_mod(*tile)

                if l == 0:
                    ff_round(0)
                with sp.Fori(0 if l else 1, ROUNDS) as q:
                    ff_round(q)
            for j in range(D // N):
                sp.wait_ge(x_ready, DEPTH * LAYER_DVE_CHUNKS - UP + j + 1)
                for t in range(T):
                    sp.dma_start(out[0, t * P:(t + 1) * P, j * N:(j + 1) * N],
                                 x_sb[:, t, j * N:(j + 1) * N]).then_inc(stored, 16)
            sp.wait_ge(stored, 16 * T * (D // N))


_INS = ["x", "c", "w_mod", "b_mod", "w_in", "w_out", "a_qnorm", "a_knorm", "a_lambda", "a_subln", "b_vnorm",
        "b_ws", "b_bias", "c_qnorm", "c_knorm", "w_ff1", "w_ff2"]


def rope_table():
    parts = []
    for dim in (DH, IDX_DH):
        inv = np.float32(1.0) / (np.float32(10000.0) ** (np.arange(0, dim, 2, dtype=np.float32) / np.float32(dim)))
        ang = np.arange(S, dtype=np.float32)[:, None] * inv[None, :].astype(np.float32)
        cos, sin = np.cos(ang), np.sin(ang)
        parts += [cos, cos, -sin, sin]
    return np.ascontiguousarray(np.concatenate(parts, axis=1), dtype=np.float32)


def kernel(**inputs):
    import concourse.bacc as bacc
    from concourse.bass_utils import run_bass_kernel_spmd

    nc = bacc.Bacc("TRN2", target_bir_lowering=False, num_devices=1, dynamic_dma_scratch_size=1024)
    arrays = {f"in_{n}_dram": np.ascontiguousarray(inputs[n]) for n in _INS}
    arrays["in_rope_dram"] = rope_table()
    args = [nc.dram_tensor(n, a.shape, mybir.dt.from_np(a.dtype), kind="ExternalInput").ap()
            for n, a in arrays.items()]
    args.append(nc.dram_tensor("out_dram", (1, S, D), F32, kind="ExternalOutput").ap())
    build_trunk(nc, *args)
    r = run_bass_kernel_spmd(nc, [arrays], core_ids=[0])
    return r.results[0]["out_dram"]
```
